# Optimizing a Trainium2 kernel written in Bass

```python
import math
import jax, jax.numpy as jnp
from jax import lax
import numpy as np

D_MODEL = 1024
BATCH = 1
SEQ = 2048
DEPTH = 1

POOL_WIDTH = D_MODEL // 2
POOL_WINDOWS = (2, 4, 8, 16)
N_POOL_GROUPS = len(POOL_WINDOWS)
POOL_GROUP = POOL_WIDTH // N_POOL_GROUPS
MAX_POOL_WINDOW = max(POOL_WINDOWS)
HEAD_DIM = 64
N_Q_HEADS = (D_MODEL - POOL_WIDTH) // HEAD_DIM
N_KV_HEADS = 2
GQA_GROUP = N_Q_HEADS // N_KV_HEADS
ATTN_WIDTH = N_Q_HEADS * HEAD_DIM
KV_WIDTH = N_KV_HEADS * HEAD_DIM
WINDOW = 128
BLOCK = 128
N_BUCKETS = 32
MAX_DISTANCE = 128
MIX_WIDTH = POOL_WIDTH + ATTN_WIDTH
IN_SPLITS = (POOL_WIDTH, 2 * POOL_WIDTH, 2 * POOL_WIDTH + ATTN_WIDTH,
             2 * POOL_WIDTH + ATTN_WIDTH + KV_WIDTH, 2 * POOL_WIDTH + ATTN_WIDTH + 2 * KV_WIDTH)
IN_WIDTH = 2 * POOL_WIDTH + 2 * ATTN_WIDTH + 2 * KV_WIDTH
DEEPNORM_ALPHA = (2.0 * DEPTH) ** 0.25
DEEPNORM_BETA = (8.0 * DEPTH) ** -0.25
LN_EPS = 1e-5
NEG_INF = -1e30

kernel_name = "hymba_pool_swa_sink_deepnorm"

def layer_norm(x, g, b):
    xf = x.astype(jnp.float32)
    mu = jnp.mean(xf, axis=-1, keepdims=True)
    var = jnp.mean(jnp.square(xf - mu), axis=-1, keepdims=True)
    y = (xf - mu) * lax.rsqrt(var + LN_EPS) * g.astype(jnp.float32) + b.astype(jnp.float32)
    return y.astype(x.dtype)

def t5_bucket(dist):
    max_exact = N_BUCKETS // 2
    is_small = dist < max_exact
    large = max_exact + (jnp.log(jnp.maximum(dist, 1).astype(jnp.float32) / max_exact)
                         / math.log(MAX_DISTANCE / max_exact) * (N_BUCKETS - max_exact)).astype(jnp.int32)
    large = jnp.minimum(large, N_BUCKETS - 1)
    return jnp.where(is_small, dist, large)

def multiscale_pool(u, pool_w, pool_scale):
    B, S, _ = u.shape
    uf = u.astype(jnp.float32)
    cs = jnp.pad(jnp.cumsum(uf, axis=1), ((0, 0), (MAX_POOL_WINDOW, 0), (0, 0)))
    t = jnp.arange(S)
    groups = []
    for gi, w in enumerate(POOL_WINDOWS):
        sl = slice(gi * POOL_GROUP, (gi + 1) * POOL_GROUP)
        window_sum = cs[:, MAX_POOL_WINDOW:, sl] - cs[:, MAX_POOL_WINDOW - w:MAX_POOL_WINDOW - w + S, sl]
        count = jnp.minimum(t + 1, w).astype(jnp.float32)[None, :, None]
        groups.append(window_sum / count - uf[..., sl])
    pooled = jnp.stack(groups, axis=2).astype(u.dtype)
    mixed = jnp.einsum('bsgc,gcd->bsgd', pooled, pool_w).reshape(B, S, POOL_WIDTH)
    return mixed * pool_scale

def sliding_window_gqa(q, k, v, sinks, rel_bias):
    B, S = q.shape[:2]
    nb = S // BLOCK
    qb = q.reshape(B, nb, BLOCK, N_KV_HEADS, GQA_GROUP, HEAD_DIM)
    kpad = jnp.pad(k, ((0, 0), (BLOCK, 0), (0, 0), (0, 0)))
    vpad = jnp.pad(v, ((0, 0), (BLOCK, 0), (0, 0), (0, 0)))
    shape_blk = (B, nb, BLOCK, N_KV_HEADS, HEAD_DIM)
    kb = jnp.concatenate([kpad[:, :S].reshape(shape_blk), kpad[:, BLOCK:].reshape(shape_blk)], axis=2)
    vb = jnp.concatenate([vpad[:, :S].reshape(shape_blk), vpad[:, BLOCK:].reshape(shape_blk)], axis=2)
    scores = jnp.einsum('bnqhgd,bnkhd->bnhgqk', qb, kb,
                        preferred_element_type=jnp.float32) * (HEAD_DIM ** -0.5)
    qi = jnp.arange(BLOCK)[:, None]
    kj = jnp.arange(2 * BLOCK)[None, :]
    dist = qi + BLOCK - kj
    blk = jnp.arange(nb)[:, None, None]
    key_abs = (blk - 1) * BLOCK + kj[None]
    valid = (dist[None] >= 0) & (dist[None] < WINDOW) & (key_abs >= 0)
    bias = rel_bias.astype(jnp.float32)[t5_bucket(jnp.clip(dist, 0, None))]
    bias = jnp.transpose(bias, (2, 0, 1)).reshape(N_KV_HEADS, GQA_GROUP, BLOCK, 2 * BLOCK)
    scores = jnp.where(valid[None, :, None, None], scores + bias[None, None], NEG_INF)
    sink = jnp.broadcast_to(sinks.astype(jnp.float32).reshape(1, 1, N_KV_HEADS, GQA_GROUP, 1, 1),
                            scores.shape[:-1] + (1,))
    probs = jax.nn.softmax(jnp.concatenate([scores, sink], axis=-1), axis=-1)[..., :-1]
    out = jnp.einsum('bnhgqk,bnkhd->bnqhgd', probs.astype(v.dtype), vb)
    return out.reshape(B, S, ATTN_WIDTH)

def hybrid_layer(x, ln_g, ln_b, w_in, pool_w, pool_scale, sinks, w_out, rel_bias):
    B, S, _ = x.shape
    h = x @ w_in
    u_pool, g_pool, q, k, v, g_attn = jnp.split(h, IN_SPLITS, axis=-1)
    y_pool = multiscale_pool(u_pool, pool_w, pool_scale) * jax.nn.silu(g_pool)
    y_attn = sliding_window_gqa(q.reshape(B, S, N_Q_HEADS, HEAD_DIM),
                                k.reshape(B, S, N_KV_HEADS, HEAD_DIM),
                                v.reshape(B, S, N_KV_HEADS, HEAD_DIM),
                                sinks, rel_bias) * jax.nn.silu(g_attn)
    y = jnp.concatenate([y_pool, y_attn], axis=-1) @ w_out
    return layer_norm(DEEPNORM_ALPHA * x + y, ln_g, ln_b)

def setup_inputs(seed: int = 0) -> dict:
    key = jax.random.key(seed)
    ks = jax.random.split(key, 10)
    f32 = jnp.float32
    x = jax.random.normal(ks[0], (BATCH, SEQ, D_MODEL), f32)
    ln_g = 1.0 + 0.02 * jax.random.normal(ks[1], (DEPTH, D_MODEL), f32)
    ln_b = 0.02 * jax.random.normal(ks[2], (DEPTH, D_MODEL), f32)
    col_scale = jnp.ones((IN_WIDTH,), f32).at[IN_SPLITS[3]:IN_SPLITS[4]].set(DEEPNORM_BETA)
    w_in = jax.random.normal(ks[3], (DEPTH, D_MODEL, IN_WIDTH), f32) * (D_MODEL ** -0.5) * col_scale
    pool_w = jax.random.normal(ks[4], (DEPTH, N_POOL_GROUPS, POOL_GROUP, POOL_GROUP), f32) * (POOL_GROUP ** -0.5)
    pool_scale = 1.0 + 0.02 * jax.random.normal(ks[5], (DEPTH, POOL_WIDTH), f32)
    sinks = 0.5 * jax.random.normal(ks[6], (DEPTH, N_Q_HEADS), f32)
    w_out = jax.random.normal(ks[7], (DEPTH, MIX_WIDTH, D_MODEL), f32) * (MIX_WIDTH ** -0.5) * DEEPNORM_BETA
    rel_bias = 0.5 * jax.random.normal(ks[8], (N_BUCKETS, N_Q_HEADS), f32)
    return {"x": x, "ln_g": ln_g, "ln_b": ln_b, "w_in": w_in, "pool_w": pool_w,
            "pool_scale": pool_scale, "sinks": sinks, "w_out": w_out, "rel_bias": rel_bias}

def reference(x, ln_g, ln_b, w_in, pool_w, pool_scale, sinks, w_out, rel_bias):
    for layer in range(DEPTH):
        x = hybrid_layer(x, ln_g[layer], ln_b[layer], w_in[layer], pool_w[layer],
                         pool_scale[layer], sinks[layer], w_out[layer], rel_bias)
    return x


_drawn_inputs = setup_inputs


def setup_inputs(seed=0):
    import zlib

    import numpy as np

    out = dict(_drawn_inputs(seed))
    spreads = {}
    factors = {'ln_b': 2.781, 'pool_scale': 8.0, 'sinks': 8.0, 'rel_bias': 7.143}
    for name, (base, spread) in spreads.items():
        noise = np.random.default_rng([zlib.crc32(name.encode()), seed]).standard_normal(out[name].shape)
        drawn = base * np.exp(spread * noise) if base else spread * noise
        out[name] = __import__('jax').numpy.asarray(drawn.astype(out[name].dtype))
    for name, factor in factors.items():
        out[name] = (out[name] * factor).astype(out[name].dtype)
    return out
```

```python
import concourse.bass as bass
from concourse import mybir
from contextlib import ExitStack

F32 = mybir.dt.float32
F32R = mybir.dt.float32r
ALU = mybir.AluOpType
ACT = mybir.ActivationFunctionType
AX = mybir.AxisListType

P = 128
D = 1024
SEQ = 2048
CH = 512
CHUNKS = SEQ // CH
KT = D // P
BLOCKS = CH // P
HD = 64
HEADS = 8
KV = 2
GQ = HEADS // KV
GROUPS = 4
HALO = 16
BUCKETS = 32
BIAS_ROW = 3 * P
NEG_INF = -1e30
ALPHA = 2.0 ** 0.25
LN_EPS = 1e-5
SCALE = HD ** -0.5

TILES = (["k", "v"] + [f"q{t}" for t in range(4)] + [f"a{t}" for t in range(4)]
         + [x for g in (3, 2, 1, 0) for x in (f"u{g}", f"p{g}")])
NT = len(TILES)
PAIRS = (1, 0, 2, 3)
SLOTS = [(n, kp) for n in range(2) for kp in PAIRS]
NS = len(SLOTS)
NW = NT + NS
ITEMS = ["k", "v", "q0", "q1", "q2", "q3", "a0", "a1", "a2", "a3",
         "u3", "p3", "u2", "m3", "p2", "u1", "m2", "p1", "u0", "m1", "p0", "m0"]
NI = len(ITEMS)
NDONE = NI + NS
AFTER = {"u2": "m3", "u1": "m2", "u0": "m1", "p0": "m0"}
GATES = [x for x in TILES if x[0] in "ap"]
POOL_ORDER = [3, 2, 1, 0]
UNITS = [(b, g) for b in range(BLOCKS) for g in range(KV)]
NU = len(UNITS)
STEP0 = TILES.index("q3")
START = [0, 3, 6, 9, 12, 15, 18, 21]


def at(delay):
    return {s + delay: n for n, s in enumerate(START)}


SCORES_AT, EXP_AT, NORM_AT, TRANSPOSE_AT, VALUES_AT, MIX_AT = at(0), at(1), at(2), at(4), at(7), at(8)
WINDOW_STEPS = {3: 4, 2: 3, 1: 2, 0: 1}


def step_of(i, half):
    s = 2 * (i - STEP0) + half
    return s if s >= 0 else None


def done(name):
    return ITEMS.index(name) + 1


def tile_done(i):
    if i >= NW:
        return NDONE + tile_done(i - NW)
    return done(TILES[i]) if i < NT else NI + (i - NT) + 1


def window_count(group, k):
    before = POOL_ORDER[:POOL_ORDER.index(group)]
    return sum(WINDOW_STEPS[g] + 1 for g in before) + k


NWIN = sum(WINDOW_STEPS.values()) + GROUPS


def hybrid_layer(nc, x_t, x_rows, weights, pool_w, pool_scale, sinks, rel_bias, ln_g, ln_b,
                 buckets, identity, band_masks, first_counts, scratch, out):
    ctx = ExitStack()
    with ctx:
        def sb(name, shape, dt=F32):
            return ctx.enter_context(nc.sbuf_tensor(name, shape, dt))

        def sem(name):
            return ctx.enter_context(nc.semaphore(name))

        NX = 4
        x_stage = sb("x_stage", [P, NX, CH])
        x_hi = sb("x_hi", [P, KT, CH], F32R)
        x_lo = sb("x_lo", [P, KT, CH], F32R)
        w_stage = sb("w_stage", [P, 2, D])
        w_hi = sb("w_hi", [P, 2, D], F32R)
        w_lo = sb("w_lo", [P, 2, D], F32R)
        pool_w_hi = sb("pool_w_hi", [P, GROUPS, P], F32R)
        pool_w_lo = sb("pool_w_lo", [P, GROUPS, P], F32R)
        q2 = sb("q2", [P, HEADS, CH], F32R)
        k_hi2 = sb("k_hi2", [P, KV, P + CH], F32R)
        k_lo2 = sb("k_lo2", [P, KV, P + CH], F32R)
        v2 = sb("v2", [P, 1 + BLOCKS, KV, P], F32R)
        v_t = sb("v_t", [P, CH])
        tanh_t = sb("tanh_t", [P, 2, CH])
        gate_a = sb("gate_a", [P, 4, CH])
        gate_p = sb("gate_p", [P, CH])
        u_ext = sb("u_ext", [P, GROUPS, HALO + CH])
        win = [sb("win_a", [P, HALO + CH]), sb("win_b", [P, HALO + CH])]
        pooled = sb("pooled", [P, CH])
        pooled_hi = sb("pooled_hi", [P, CH], F32R)
        pooled_lo = sb("pooled_lo", [P, CH], F32R)
        mix_p = sb("mix_p", [P, CH])
        mix_a = sb("mix_a", [P, 2, P])
        mix_hi = sb("mix_hi", [P, KT, CH], F32R)
        mix_lo = sb("mix_lo", [P, KT, CH], F32R)
        bias = sb("bias", [P, HEADS, 2 * P])
        scores = sb("scores", [P, GQ, 2 * P])
        probs = sb("probs", [P, GQ, P])
        pt_hi = sb("pt_hi", [P, GQ, P], F32R)
        pt_lo = sb("pt_lo", [P, GQ, P], F32R)
        band_hi = sb("band_hi", [P, 2, GQ, P], F32R)
        band_lo = sb("band_lo", [P, 2, GQ, P], F32R)
        av_sum = sb("av_sum", [P, 2, P])
        resid = sb("resid", [P, BLOCKS, D])
        ln_g_sb = sb("ln_g_sb", [P, D])
        ln_b_sb = sb("ln_b_sb", [P, D])
        ident = sb("ident", [P, P])
        masks = sb("masks", [P, 2, P])
        corr = sb("corr", [P, GROUPS, HALO])
        sinks_sb = sb("sinks_sb", [P, HEADS])
        neg_sinks = sb("neg_sinks", [P, HEADS])
        scale_sb = sb("scale_sb", [P, GROUPS])
        half_scale = sb("half_scale", [P, GROUPS])
        rel_ext = sb("rel_ext", [BUCKETS + 1, HEADS])
        onehot = pooled[0:BUCKETS + 1, 0:BIAS_ROW]
        bias_row = mix_p[0:HEADS, 0:BIAS_ROW]
        prev_mask = sb("prev_mask", [P, 1])
        row_max = sb("row_max", [P, GQ])
        neg_max = sb("neg_max", [P, GQ])
        sink_shift = sb("sink_shift", [P, GQ])
        sink_exp = sb("sink_exp", [P, GQ])
        exp_sum = sb("exp_sum", [P, GQ])
        total = sb("total", [P, GQ])
        inv_total = sb("inv_total", [P, GQ])
        stats = sb("stats", [P, BLOCKS, 2, 6])
        mean_var = sb("mean_var", [P, BLOCKS, 2])
        var_eps = sb("var_eps", [P, BLOCKS])
        minus_half = sb("minus_half", [P, BLOCKS])
        rstd = sb("rstd", [P, BLOCKS])

        acc = [ctx.enter_context(nc.psum_tensor(f"acc{i}", [P, CH], F32)) for i in range(4)]
        s_ps = ctx.enter_context(nc.psum_tensor("s_ps", [P, GQ, 2 * P], F32))
        t_ps = ctx.enter_context(nc.psum_tensor("t_ps", [P, GQ, P], F32))
        v_ps = ctx.enter_context(nc.psum_tensor("v_ps", [P, GQ, P], F32))

        consts_loaded = sem("consts_loaded")
        ln_loaded = sem("ln_loaded")
        cleared = sem("cleared")
        ext_ready = sem("ext_ready")
        row_ready = sem("row_ready")
        row_copied = sem("row_copied")
        row_stored = sem("row_stored")
        bias_loaded = sem("bias_loaded")
        derived = sem("derived")
        pool_w_high = sem("pool_w_high")
        pool_w_split = sem("pool_w_split")
        w_loaded = [sem("w_loaded0"), sem("w_loaded1")]
        w_high = sem("w_high")
        w_split = sem("w_split")
        x_loaded = [sem(f"x_loaded{i}") for i in range(NX)]
        x_high = sem("x_high")
        x_split = sem("x_split")
        pe_done = sem("pe_done")
        hi_ready = sem("hi_ready")
        low_ready = sem("low_ready")
        gate_ready = sem("gate_ready")
        scores_ready = sem("scores_ready")
        biased = sem("biased")
        first_masked = sem("first_masked")
        merged = sem("merged")
        max_ready = sem("max_ready")
        neg_max_ready = sem("neg_max_ready")
        shift_ready = sem("shift_ready")
        exp_ready = sem("exp_ready")
        total_ready = sem("total_ready")
        inv_ready = sem("inv_ready")
        probs_ready = sem("probs_ready")
        halo_k = sem("halo_k")
        halo_k_low = sem("halo_k_low")
        halo_v = sem("halo_v")
        t_ready = sem("t_ready")
        t_high = sem("t_high")
        t_low = sem("t_low")
        band_hi_ready = sem("band_hi_ready")
        band_lo_ready = sem("band_lo_ready")
        av_ready = sem("av_ready")
        av_copied = sem("av_copied")
        av_summed = sem("av_summed")
        mix_a_ready = sem("mix_a_ready")
        mix_a_high = sem("mix_a_high")
        mix_a_split = sem("mix_a_split")
        window_step = sem("window_step")
        pooled_ready = sem("pooled_ready")
        halo_u = sem("halo_u")
        pooled_high = sem("pooled_high")
        pooled_split = sem("pooled_split")
        mix_p_ready = sem("mix_p_ready")
        mix_p_high = sem("mix_p_high")
        mix_p_split = sem("mix_p_split")
        corr_reset = sem("corr_reset")
        mask_reset = sem("mask_reset")
        resid_loaded = [sem(f"resid_loaded{i}") for i in range(BLOCKS)]
        out_part = sem("out_part")
        sum_ready = sem("sum_ready")
        stats_ready = sem("stats_ready")
        stats_seen = sem("stats_seen")
        aggr_ready = sem("aggr_ready")
        var_ready = sem("var_ready")
        rstd_ready = sem("rstd_ready")
        centred = sem("centred")
        ln_done = sem("ln_done")
        out_stored = [sem(f"out_stored{i}") for i in range(BLOCKS)]

        block = ctx.enter_context(nc.Block())
        NCONST = 9

        @block.sync
        def _(sp):
            def load_w(i):
                sp.dma_start(w_stage[:, i % 2, :], weights[i % NW]).then_inc(w_loaded[i % 2], 16)

            def load_x(c, k):
                sp.dma_start(x_stage[:, k % NX, :], x_t[c, :, k, :]).then_inc(x_loaded[k % NX], 16)

            def load_rows(c, tt):
                sp.dma_start(resid[:, tt, :], x_rows[c, tt]).then_inc(resid_loaded[tt], 16)

            load_x(0, 0)
            load_w(0)
            for k in range(1, NX):
                load_x(0, k)
            load_w(1)
            for k in range(NX, KT):
                sp.wait_ge(x_split, k - NX + 1)
                load_x(0, k)

            sp.wait_ge(row_copied, 1)
            sp.dma_start(scratch.rearrange("(h i m) -> h i m", h=HEADS, i=P),
                         bias_row.unsqueeze(1).broadcast_to([HEADS, P, BIAS_ROW])).then_inc(row_stored, 16)
            sp.wait_ge(row_stored, 16)
            for h in range(HEADS):
                at = h * P * BIAS_ROW + P - 1
                skewed = scratch[at:at + P * (BIAS_ROW - 1)].rearrange("(i m) -> i m", i=P)
                sp.dma_start(bias[:, h, :], skewed[:, 0:2 * P]).then_inc(bias_loaded, 16)

            HEAD = 4

            def stream(c, tiles, last):
                for i in tiles:
                    if not (last and i + 2 >= NW):
                        sp.wait_ge(w_split, c * NW + i + 1)
                        load_w(i + 2)
                    if not last and NT - 6 <= i < NT - 2:
                        load_x(c + 1, i - (NT - 6))
                    if not last and NT + 2 <= i < NT + 2 + KT - NX:
                        k = i - NT - 2 + NX
                        sp.wait_ge(x_split, c * KT + KT + k - NX + 1)
                        load_x(c + 1, k)

            def store_rows(c):
                for tt in range(BLOCKS):
                    sp.wait_ge(ln_done, c * BLOCKS + tt + 1)
                    sp.dma_start(out[c, tt], resid[:, tt, :]).then_inc(out_stored[tt], 16)

            stream(0, range(HEAD), False)
            sp.dma_start(ln_g_sb[:, :], ln_g).then_inc(ln_loaded, 16)
            sp.dma_start(ln_b_sb[:, :], ln_b).then_inc(ln_loaded, 16)
            for tt in range(BLOCKS):
                load_rows(0, tt)
            with sp.Fori(0, CHUNKS - 1) as c:
                stream(c, range(HEAD, NW), False)
                stream(c + 1, range(HEAD), False)
                store_rows(c)
                for tt in range(BLOCKS):
                    sp.wait_ge(out_stored[tt], (c + 1) * 16)
                    load_rows(c + 1, tt)
            stream(CHUNKS - 1, range(HEAD, NW), True)
            store_rows(CHUNKS - 1)
            for tt in range(BLOCKS):
                sp.wait_ge(out_stored[tt], CHUNKS * 16)

        @block.tensor
        def _(pe):
            mm = nc.tensor.matmul

            pe.wait_ge(consts_loaded, NCONST * 16)
            pe.wait_ge(ext_ready, 1)
            mm(v_ps[0:HEADS, 0:3, :], rel_ext[:, :], onehot, start=True, stop=True).then_inc(row_ready, 1)

            def bank_free(c, idx):
                if idx < 4:
                    pe.wait_ge(sum_ready, c * 2 * BLOCKS + BLOCKS + idx + 1)
                    return
                name = ITEMS[idx - 4] if idx < NI + 4 else None
                kind = name[0]
                if kind in "kq":
                    n = 0 if kind == "k" else 1 + int(name[1])
                    pe.wait_ge(low_ready, c * 5 + n + 1)
                elif kind in "vu":
                    pe.wait_ge(hi_ready, c * NT + TILES.index(name) + 1)
                elif kind in "ap":
                    pe.wait_ge(gate_ready, c * 8 + GATES.index(name) + 1)
                else:
                    pe.wait_ge(mix_p_ready, c * GROUPS + POOL_ORDER.index(int(name[1])) + 1)

            def tile_half(c, i, half):
                idx = ITEMS.index(TILES[i])
                w, to = i % 2, acc[idx % 4][:, :]
                if half == 0:
                    bank_free(c, idx)
                    pe.wait_ge(w_split, c * NW + i + 1)
                for k in range(4 * half, 4 * half + 4):
                    if i == 0:
                        pe.wait_ge(x_split, c * KT + k + 1)
                    cols = slice(k * P, (k + 1) * P)
                    mm(to, w_hi[:, w, cols], x_hi[:, k, :], start=(k == 0), stop=False)
                    mm(to, w_hi[:, w, cols], x_lo[:, k, :], start=False, stop=False)
                    last = mm(to, w_lo[:, w, cols], x_hi[:, k, :], start=False, stop=(k == KT - 1))
                if half == 1:
                    last.then_inc(pe_done, 1)

            def pool_product(c, name):
                g = int(name[1])
                idx = ITEMS.index(name)
                to = acc[idx % 4][:, :]
                bank_free(c, idx)
                pe.wait_ge(pooled_split, c * GROUPS + POOL_ORDER.index(g) + 1)
                if name == "m3":
                    pe.wait_ge(pool_w_split, 1)
                mm(to, pool_w_hi[:, g, :], pooled_hi[:, :], start=True, stop=False)
                mm(to, pool_w_hi[:, g, :], pooled_lo[:, :], start=False, stop=False)
                mm(to, pool_w_lo[:, g, :], pooled_hi[:, :], start=False, stop=True).then_inc(pe_done, 1)

            def transpose_values(c):
                pe.wait_ge(hi_ready, c * NT + 2)
                for b in range(BLOCKS):
                    last = nc.tensor.transpose(t_ps[:, b, :], v_t[:, b * P:(b + 1) * P], ident[:, :])
                last.then_inc(t_ready, 1)

            def unit_scores(c, n):
                b, g = UNITS[n]
                if b == 0:
                    pe.wait_ge(low_ready, c * 5 + 3 + 2 * g)
                if n:
                    pe.wait_ge(biased, c * NU + n)
                for h in range(GQ):
                    to = s_ps[:, h, :]
                    q = q2[:, g * GQ + h, b * P:(b + 1) * P]
                    mm(to, q, k_hi2[:, g, b * P:b * P + 2 * P], start=True, stop=False)
                    last = mm(to, q, k_lo2[:, g, b * P:b * P + 2 * P], start=False, stop=True)
                last.then_inc(scores_ready, 1)

            def unit_transpose(c, n):
                pe.wait_ge(probs_ready, c * NU + n + 1)
                pe.wait_ge(t_low, c * (NU + 1) + n + 1)
                for h in range(GQ):
                    last = nc.tensor.transpose(t_ps[:, h, :], probs[:, h, :], ident[:, :])
                last.then_inc(t_ready, 1)

            def unit_values(c, n):
                b, g = UNITS[n]
                pe.wait_ge(band_hi_ready, c * NU + n + 1)
                pe.wait_ge(band_lo_ready, c * NU + n + 1)
                if n:
                    pe.wait_ge(av_summed, c * NU + n)
                for j in range(2):
                    v = v2[:, b + j, g, :]
                    mm(v_ps[:, :, :], v, band_hi[:, j, :, :], start=(j == 0), stop=False)
                    last = mm(v_ps[:, :, :], v, band_lo[:, j, :, :], start=False, stop=(j == 1))
                last.then_inc(av_ready, 1)

            def out_half(c, s, half):
                n, kp = SLOTS[s]
                i = NT + s
                w = i % 2
                if half == 0:
                    pe.wait_ge(w_split, c * NW + i + 1)
                    if kp < 2:
                        g = 2 * kp
                        pe.wait_ge(mix_p_split, c * GROUPS + POOL_ORDER.index(g) + 1)
                    else:
                        pe.wait_ge(mix_a_split, c * NU + NU - (kp == 2))
                order = ([(tt, h) for tt in (2 * half, 2 * half + 1) for h in range(2)] if kp == PAIRS[-1]
                         else [(tt, half) for tt in range(BLOCKS)])
                for tt, h in order:
                    k = 2 * kp + h
                    first = kp == PAIRS[0] and h == 0
                    final = kp == PAIRS[-1] and h == 1
                    if first and n == 0:
                        bank_free_out(c, tt)
                    if first and n == 1:
                        pe.wait_ge(sum_ready, c * 2 * BLOCKS + 2 * BLOCKS + tt + 1)
                    to = acc[tt][:, :]
                    rows = slice(tt * P, (tt + 1) * P)
                    cols = slice(h * CH, (h + 1) * CH)
                    mm(to, mix_hi[:, k, rows], w_hi[:, w, cols], start=first, stop=False)
                    mm(to, mix_hi[:, k, rows], w_lo[:, w, cols], start=False, stop=False)
                    last = mm(to, mix_lo[:, k, rows], w_hi[:, w, cols], start=False, stop=final)
                    if final and tt < BLOCKS - 1:
                        last.then_inc(out_part, 1)
                if half == 1:
                    last.then_inc(pe_done, 1)

            def bank_free_out(c, tt):
                idx = max(j for j in range(NI) if j % 4 == tt)
                bank_free(c, idx + 4)

            def attention(c, s):
                if s is None:
                    return
                if s in TRANSPOSE_AT:
                    unit_transpose(c, TRANSPOSE_AT[s])
                if s in SCORES_AT:
                    unit_scores(c, SCORES_AT[s])
                if s in VALUES_AT:
                    unit_values(c, VALUES_AT[s])

            def chunk(c, last):
                for i in range(NW):
                    for half in range(2):
                        if i < NT:
                            tile_half(c, i, half)
                        else:
                            out_half(c, i - NT, half)
                        attention(c, step_of(i, half))
                    if i == 2:
                        transpose_values(c)
                    if i < NT and TILES[i] in AFTER:
                        pool_product(c, AFTER[TILES[i]])

            with pe.Fori(0, CHUNKS - 1) as c:
                chunk(c, False)
            chunk(CHUNKS - 1, True)

        @block.scalar
        def _(act):
            copy = lambda o, i: nc.scalar.activation(o, i, ACT.Copy)

            for o, i in ((rel_ext[0:BUCKETS, :], rel_bias), (onehot, buckets), (ident[:, :], identity),
                         (sinks_sb[:, :], sinks), (scale_sb[:, :], pool_scale),
                         (masks[:, :, :], band_masks), (corr[:, :, :], first_counts),
                         (mix_a[:, :, :], pool_w[:, 0:2, :]), (av_sum[:, :, :], pool_w[:, 2:4, :])):
                act.dma_start(o, i).then_inc(consts_loaded, 16)

            def split_w(c, i):
                if i >= 2:
                    act.wait_ge(pe_done, c * NDONE + tile_done(i - 2))
                act.wait_ge(w_loaded[i % 2], (c * (NW // 2) + i // 2 + 1) * 16)
                copy(w_hi[:, i % 2, :], w_stage[:, i % 2, :]).then_inc(w_high, 1)

            def split_x(c, k):
                act.wait_ge(x_loaded[k % NX], (c * (KT // NX) + k // NX + 1) * 16)
                copy(x_hi[:, k, :], x_stage[:, k % NX, :]).then_inc(x_high, 1)

            split_x(0, 0)
            split_w(0, 0)
            for k in range(1, NX):
                split_x(0, k)
            split_w(0, 1)
            act.wait_ge(row_ready, 1)
            copy(bias_row, v_ps[0:HEADS, 0:3, :].rearrange("h a m -> h (a m)")).then_inc(row_copied, 1)
            for k in range(NX, KT):
                split_x(0, k)
            act.wait_ge(consts_loaded, NCONST * 16)
            copy(pool_w_hi[:, 0:2, :], mix_a[:, :, :])
            copy(pool_w_hi[:, 2:4, :], av_sum[:, :, :]).then_inc(pool_w_high, 1)
            split_w(0, 2)
            act.wait_ge(cleared, 1)

            def evacuate(c, i):
                name = TILES[i]
                kind, t = name[0], int(name[1:] or 0)
                act.wait_ge(pe_done, c * NDONE + done(name))
                src = acc[ITEMS.index(name) % 4]
                if kind == "k":
                    copy(k_hi2[:, :, 0:P], k_hi2[:, :, CH:CH + P].bitcast(F32)).then_inc(halo_k, 1)
                    act.wait_ge(halo_k, c + 1)
                    for a in range(KV):
                        for r in range(2):
                            last = copy(k_hi2[r * HD:(r + 1) * HD, a, P:], src[a * HD:(a + 1) * HD, :])
                elif kind == "v":
                    last = copy(v_t[:, :], src[:, :])
                elif kind == "q":
                    for a in range(2):
                        last = copy(q2[0:HD, 2 * t + a, :], src[a * HD:(a + 1) * HD, :])
                elif kind == "u":
                    copy(u_ext[:, t, 0:HALO], u_ext[:, t, CH:CH + HALO]).then_inc(halo_u, 1)
                    act.wait_ge(halo_u, c * GROUPS + POOL_ORDER.index(t) + 1)
                    last = copy(u_ext[:, t, HALO:], src[:, :])
                else:
                    m = GATES.index(name)
                    if m >= 2:
                        act.wait_ge(gate_ready, c * 8 + m - 1)
                    last = nc.scalar.activation(tanh_t[:, m % 2, :], src[:, :], ACT.Tanh, scale=0.5)
                last.then_inc(hi_ready, 1)

            def split_values(c):
                act.wait_ge(t_ready, c * (NU + 1) + 1)
                copy(v2[:, 0, :, :], v2[:, BLOCKS, :, :].bitcast(F32)).then_inc(halo_v, 1)
                act.wait_ge(halo_v, c + 1)
                copy(v2[:, 1:, :, 0:HD], t_ps[:, :, :].rearrange("p b (g d) -> p b g d", g=KV)).then_inc(t_high, 1)

            def unit_exp(c, n):
                act.wait_ge(shift_ready, c * NU + n + 1)
                if n:
                    act.wait_ge(total_ready, c * NU + n)
                act.wait_ge(t_ready, c * (NU + 1) + n + 1)
                nc.scalar.activation(sink_exp[:, :], sink_shift[:, :], ACT.Exp)
                for h in range(GQ):
                    last = nc.scalar.activation(probs[:, h, :], scores[:, h, 0:P], ACT.Exp,
                                                bias=neg_max[:, h:h + 1], accum_out=exp_sum[:, h:h + 1])
                last.then_inc(exp_ready, 1)

            def unit_pt_high(c, n):
                act.wait_ge(t_ready, c * (NU + 1) + n + 2)
                if n:
                    act.wait_ge(band_hi_ready, c * NU + n)
                copy(pt_hi[:, :, :], t_ps[:, :, :]).then_inc(t_high, 1)

            def unit_av_copy(c, n):
                act.wait_ge(av_ready, c * NU + n + 1)
                copy(v_t[0:HD, :], v_ps[HD:P, :, :].rearrange("p h q -> p (h q)")).then_inc(av_copied, 1)

            def unit_mix(c, n):
                b, g = UNITS[n]
                act.wait_ge(mix_a_ready, c * NU + n + 1)
                copy(mix_hi[:, 4 + 2 * g:6 + 2 * g, b * P:(b + 1) * P], mix_a[:, :, :]).then_inc(mix_a_high, 1)

            def pooled_part(c, g):
                n = POOL_ORDER.index(g)
                act.wait_ge(pooled_ready, c * GROUPS + n + 1)
                if n:
                    act.wait_ge(pe_done, c * NDONE + done(f"m{POOL_ORDER[n - 1]}"))
                copy(pooled_hi[:, :], pooled[:, :]).then_inc(pooled_high, 1)

            def mix_p_part(c, g):
                n = POOL_ORDER.index(g)
                act.wait_ge(mix_p_ready, c * GROUPS + n + 1)
                copy(mix_hi[:, g, :], mix_p[:, :]).then_inc(mix_p_high, 1)

            def attention(c, s):
                if s is None:
                    return
                if s in TRANSPOSE_AT:
                    unit_pt_high(c, TRANSPOSE_AT[s])
                if s in VALUES_AT:
                    unit_av_copy(c, VALUES_AT[s])
                if s in EXP_AT:
                    unit_exp(c, EXP_AT[s])
                if s in MIX_AT:
                    unit_mix(c, MIX_AT[s])

            def chunk(c, last):
                for i in range(NW):
                    if 1 <= i <= NT and TILES[i - 1] in AFTER:
                        mix_p_part(c, int(AFTER[TILES[i - 1]][1]))
                    if i < NT and TILES[i] == "p0":
                        pooled_part(c, 0)
                    attention(c, step_of(i, 0))
                    if i < NT:
                        evacuate(c, i)
                    if 1 <= i < NW - 1 - (1 if last else 0):
                        split_w(c, i + 2)
                    attention(c, step_of(i, 1))
                    if i < NT and TILES[i] in ("p3", "p2", "p1"):
                        pooled_part(c, int(TILES[i][1]))
                    if i == 3:
                        split_values(c)
                    if not last and i >= NT:
                        if i == NT:
                            act.wait_ge(pe_done, c * NDONE + NI)
                        split_x(c + 1, i - NT)
                if not last:
                    split_w(c, NW + 1)
                    split_w(c, NW + 2)

            with act.Fori(0, CHUNKS - 1) as c:
                chunk(c, False)
            chunk(CHUNKS - 1, True)

        @block.vector
        def _(dve):
            tt_ = nc.vector.tensor_tensor
            stt = nc.vector.scalar_tensor_tensor

            dve.sem_inc(sum_ready, 2 * BLOCKS)
            dve.sem_inc(corr_reset, 1)
            nc.vector.memset(prev_mask[:, :], NEG_INF).then_inc(mask_reset, 1)
            nc.vector.memset(rel_ext[BUCKETS:BUCKETS + 1, :], 1.0).then_inc(ext_ready, 1)

            def split_x(c, k):
                dve.wait_ge(x_high, c * KT + k + 1)
                tt_(out=x_lo[:, k, :], in0=x_stage[:, k % NX, :], in1=x_hi[:, k, :].bitcast(F32),
                    op=ALU.subtract).then_inc(x_split, 1)

            def split_w(c, i):
                dve.wait_ge(w_high, c * NW + i + 1)
                tt_(out=w_lo[:, i % 2, :], in0=w_stage[:, i % 2, :], in1=w_hi[:, i % 2, :].bitcast(F32),
                    op=ALU.subtract).then_inc(w_split, 1)

            split_x(0, 0)
            split_w(0, 0)
            for k in range(1, NX):
                split_x(0, k)
            split_w(0, 1)
            for k in range(NX, KT):
                split_x(0, k)
            dve.wait_ge(pool_w_high, 1)
            tt_(out=pool_w_lo[:, 0:2, :], in0=mix_a[:, :, :], in1=pool_w_hi[:, 0:2, :].bitcast(F32), op=ALU.subtract)
            tt_(out=pool_w_lo[:, 2:4, :], in0=av_sum[:, :, :], in1=pool_w_hi[:, 2:4, :].bitcast(F32),
                op=ALU.subtract).then_inc(pool_w_split, 1)
            nc.vector.tensor_scalar(neg_sinks[:, :], sinks_sb[:, :], -1.0, None, ALU.mult).then_inc(derived, 1)
            nc.vector.tensor_scalar(half_scale[:, :], scale_sb[:, :], 0.5, None, ALU.mult).then_inc(derived, 1)
            dve.wait_ge(derived, 2)
            split_w(0, 2)
            dve.wait_ge(cleared, 1)

            def evacuate(c, i):
                name = TILES[i]
                kind, t = name[0], int(name[1:] or 0)
                src = acc[ITEMS.index(name) % 4]
                if kind in "vu":
                    return
                dve.wait_ge(hi_ready, c * NT + i + 1)
                if kind == "k":
                    nc.vector.tensor_copy(k_lo2[:, :, 0:P], k_lo2[:, :, CH:CH + P].bitcast(F32)).then_inc(halo_k_low, 1)
                    dve.wait_ge(halo_k_low, c + 1)
                    for a in range(KV):
                        for r in range(2):
                            rows = slice(r * HD, (r + 1) * HD)
                            last = tt_(out=k_lo2[rows, a, P:], in0=src[a * HD:(a + 1) * HD, :],
                                       in1=k_hi2[rows, a, P:].bitcast(F32), op=ALU.subtract)
                    last.then_inc(low_ready, 1)
                elif kind == "q":
                    for a in range(2):
                        last = tt_(out=q2[HD:P, 2 * t + a, :], in0=src[a * HD:(a + 1) * HD, :],
                                   in1=q2[0:HD, 2 * t + a, :].bitcast(F32), op=ALU.subtract)
                    last.then_inc(low_ready, 1)
                else:
                    m = GATES.index(name)
                    to = gate_a[:, t, :] if kind == "a" else gate_p[:, :]
                    stt(out=to, in0=tanh_t[:, m % 2, :], scalar=1.0, in1=src[:, :],
                        op0=ALU.add, op1=ALU.mult).then_inc(gate_ready, 1)

            def split_values(c):
                dve.wait_ge(t_high, c * (NU + 1) + 1)
                tt_(out=v2[:, 1:, :, HD:P], in0=t_ps[:, :, :].rearrange("p b (g d) -> p b g d", g=KV),
                    in1=v2[:, 1:, :, 0:HD].bitcast(F32), op=ALU.subtract).then_inc(t_low, 1)

            def unit_max(c, n):
                b, g = UNITS[n]
                heads = slice(g * GQ, (g + 1) * GQ)
                dve.wait_ge(scores_ready, c * NU + n + 1)
                if n == 0:
                    dve.wait_ge(bias_loaded, HEADS * 16)
                stt(out=scores[:, :, :], in0=s_ps[:, :, :], scalar=SCALE, in1=bias[:, heads, :],
                    op0=ALU.mult, op1=ALU.add).then_inc(biased, 1)
                dve.wait_ge(biased, c * NU + n + 1)
                if b == 0:
                    dve.wait_ge(mask_reset, c + 1)
                    nc.vector.tensor_scalar(scores[:, :, 0:P], scores[:, :, 0:P], prev_mask[:, 0:1], None,
                                            ALU.add).then_inc(first_masked, 1)
                    dve.wait_ge(first_masked, c * KV + g + 1)
                tt_(out=scores[:, :, 0:P], in0=scores[:, :, 0:P], in1=scores[:, :, P:], op=ALU.max).then_inc(merged, 1)
                dve.wait_ge(merged, c * NU + n + 1)
                nc.vector.tensor_reduce(out=row_max[:, :], in_=scores[:, :, 0:P], op=ALU.max, axis=AX.X).then_inc(max_ready, 1)
                dve.wait_ge(max_ready, c * NU + n + 1)
                stt(out=neg_max[:, :], in0=row_max[:, :], scalar=-1.0, in1=neg_sinks[:, heads],
                    op0=ALU.mult, op1=ALU.min).then_inc(neg_max_ready, 1)
                dve.wait_ge(neg_max_ready, c * NU + n + 1)
                tt_(out=sink_shift[:, :], in0=sinks_sb[:, heads], in1=neg_max[:, :], op=ALU.add).then_inc(shift_ready, 1)

            def unit_normalise(c, n):
                dve.wait_ge(exp_ready, c * NU + n + 1)
                tt_(out=total[:, :], in0=exp_sum[:, :], in1=sink_exp[:, :], op=ALU.add).then_inc(total_ready, 1)
                dve.wait_ge(total_ready, c * NU + n + 1)
                nc.vector.reciprocal(inv_total[:, :], total[:, :]).then_inc(inv_ready, 1)
                dve.wait_ge(inv_ready, c * NU + n + 1)
                tt_(out=probs[:, :, :], in0=probs[:, :, :],
                    in1=inv_total[:, :].unsqueeze(2).broadcast_to([P, GQ, P]), op=ALU.mult).then_inc(probs_ready, 1)

            def unit_pt_low(c, n):
                dve.wait_ge(t_high, c * (NU + 1) + n + 2)
                if n:
                    dve.wait_ge(band_lo_ready, c * NU + n)
                tt_(out=pt_lo[:, :, :], in0=t_ps[:, :, :], in1=pt_hi[:, :, :].bitcast(F32),
                    op=ALU.subtract).then_inc(t_low, 1)

            def unit_gate(c, n):
                b, g = UNITS[n]
                dve.wait_ge(av_copied, c * NU + n + 1)
                low = v_t[0:HD, :].rearrange("p (t a q) -> p t a q", t=2, a=2)
                high = v_ps[0:HD, :, :].rearrange("p (t a) q -> p t a q", a=2)
                for a in range(2):
                    last = tt_(out=av_sum[a * HD:(a + 1) * HD, :, :], in0=high[:, :, a, :], in1=low[:, :, a, :], op=ALU.add)
                last.then_inc(av_summed, 1)
                dve.wait_ge(av_summed, c * NU + n + 1)
                if b == 0:
                    dve.wait_ge(gate_ready, c * 8 + 2 * g + 2)
                if n:
                    dve.wait_ge(mix_a_split, c * NU + n)
                stt(out=mix_a[:, :, :], in0=av_sum[:, :, :], scalar=0.5,
                    in1=gate_a[:, 2 * g:2 * g + 2, b * P:(b + 1) * P], op0=ALU.mult, op1=ALU.mult).then_inc(mix_a_ready, 1)

            def pooled_diff(c, g):
                n = POOL_ORDER.index(g)
                dve.wait_ge(window_step, c * NWIN + window_count(g, WINDOW_STEPS[g] + 1))
                if n:
                    dve.wait_ge(pooled_split, c * GROUPS + n)
                w = win[(WINDOW_STEPS[g] + 1) % 2]
                stt(out=pooled[:, :], in0=w[:, HALO:], scalar=1.0 / 2 ** (g + 1), in1=u_ext[:, g, HALO:],
                    op0=ALU.mult, op1=ALU.subtract).then_inc(pooled_ready, 1)

            def mix_p_gate(c, g):
                n = POOL_ORDER.index(g)
                dve.wait_ge(pe_done, c * NDONE + done(f"m{g}"))
                dve.wait_ge(gate_ready, c * 8 + GATES.index(f"p{g}") + 1)
                if n:
                    dve.wait_ge(mix_p_split, c * GROUPS + n)
                src = acc[ITEMS.index(f"m{g}") % 4]
                stt(out=mix_p[:, :], in0=src[:, :], scalar=half_scale[:, g:g + 1], in1=gate_p[:, :],
                    op0=ALU.mult, op1=ALU.mult).then_inc(mix_p_ready, 1)

            def residual(c, n, tt):
                if tt < BLOCKS - 1:
                    dve.wait_ge(out_part, c * 6 + n * 3 + tt + 1)
                else:
                    dve.wait_ge(pe_done, c * NDONE + NI + 4 * n + 4)
                if n == 0:
                    dve.wait_ge(resid_loaded[tt], (c + 1) * 16)
                part = resid[:, tt, n * CH:(n + 1) * CH]
                stt(out=part, in0=part, scalar=ALPHA, in1=acc[tt][:, :], op0=ALU.mult, op1=ALU.add).then_inc(sum_ready, 1)
                dve.wait_ge(sum_ready, c * 2 * BLOCKS + 2 * BLOCKS + n * BLOCKS + tt + 1)
                nc.vector.bn_stats(out=stats[:, tt, n, :], in_=part).then_inc(stats_ready, 1)

            def norm_scalars(c):
                dve.wait_ge(stats_ready, (c + 1) * 2 * BLOCKS)
                dve.sem_inc(stats_seen, 1)
                for tt in range(BLOCKS):
                    last = nc.vector.bn_aggr(out=mean_var[:, tt, :], in_=stats[:, tt, :, :])
                last.then_inc(aggr_ready, 1)
                dve.wait_ge(aggr_ready, c + 1)
                nc.vector.tensor_scalar(var_eps[:, :], mean_var[:, :, 1], LN_EPS, None, ALU.add).then_inc(var_ready, 1)

            def normalise(c, tt):
                rows = resid[:, tt, :]
                if tt == 0:
                    dve.wait_ge(ln_loaded, 2 * 16)
                    dve.wait_ge(rstd_ready, c + 1)
                stt(out=rows, in0=rows, scalar=mean_var[:, tt, 0:1], in1=ln_g_sb[:, :],
                    op0=ALU.subtract, op1=ALU.mult).then_inc(centred, 1)
                dve.wait_ge(centred, c * BLOCKS + tt + 1)
                stt(out=rows, in0=rows, scalar=rstd[:, tt:tt + 1], in1=ln_b_sb[:, :],
                    op0=ALU.mult, op1=ALU.add).then_inc(ln_done, 1)

            def attention(c, s):
                if s is None:
                    return
                if s in NORM_AT:
                    unit_normalise(c, NORM_AT[s])
                if s in TRANSPOSE_AT:
                    unit_pt_low(c, TRANSPOSE_AT[s])
                if s in SCORES_AT:
                    unit_max(c, SCORES_AT[s])
                if s in VALUES_AT:
                    unit_gate(c, VALUES_AT[s])

            def chunk(c, last):
                for i in range(NW):
                    if i < NT and TILES[i] == "p0":
                        pooled_diff(c, 0)
                    attention(c, step_of(i, 0))
                    if i < NT:
                        evacuate(c, i)
                    if i == NT + 3:
                        for tt in range(BLOCKS):
                            residual(c, 0, tt)
                    if 1 <= i < NW - 1 - (1 if last else 0):
                        split_w(c, i + 2)
                    attention(c, step_of(i, 1))
                    if i < NT and TILES[i] in ("p3", "p2", "p1"):
                        pooled_diff(c, int(TILES[i][1]))
                    if i == 3:
                        split_values(c)
                    if i < NT and TILES[i] in AFTER:
                        mix_p_gate(c, int(AFTER[TILES[i]][1]))
                    if not last and i >= NT:
                        split_x(c + 1, i - NT)
                nc.vector.memset(prev_mask[:, :], 0.0).then_inc(mask_reset, 1)
                dve.wait_ge(window_step, c * NWIN + NWIN)
                nc.vector.memset(corr[:, :, :], 1.0).then_inc(corr_reset, 1)
                for tt in range(BLOCKS):
                    residual(c, 1, tt)
                norm_scalars(c)
                if not last:
                    split_w(c, NW + 1)
                normalise(c, 0)
                normalise(c, 1)
                if not last:
                    split_w(c, NW + 2)
                normalise(c, 2)
                normalise(c, 3)

            with dve.Fori(0, CHUNKS - 1) as c:
                chunk(c, False)
            chunk(CHUNKS - 1, True)

        @block.gpsimd
        def _(pool):
            tt_ = nc.gpsimd.tensor_tensor

            nc.gpsimd.memset(k_hi2[:, :, :].bitcast(F32), 0.0)
            nc.gpsimd.memset(k_lo2[:, :, :].bitcast(F32), 0.0)
            nc.gpsimd.memset(v2[:, :, :, :].bitcast(F32), 0.0)
            nc.gpsimd.memset(u_ext[:, :, CH:CH + HALO], 0.0)
            nc.gpsimd.memset(minus_half[:, :], -0.5).then_inc(cleared, 1)
            pool.wait_ge(cleared, 1)

            pool.wait_ge(consts_loaded, NCONST * 16)

            def window_sums(c, g):
                pool.wait_ge(hi_ready, c * NT + TILES.index(f"u{g}") + 1)
                steps = WINDOW_STEPS[g]
                src, lo = u_ext[:, g, :], 0
                for k in range(steps):
                    d = 1 << k
                    lo += d
                    start = HALO if k == steps - 1 else lo
                    dst = win[(steps + 1 + (steps - 1 - k)) % 2]
                    if k:
                        pool.wait_ge(window_step, c * NWIN + window_count(g, k))
                    tt_(out=dst[:, start:], in0=src[:, start:], in1=src[:, start - d:HALO + CH - d],
                        op=ALU.add).then_inc(window_step, 1)
                    src = dst
                pool.wait_ge(window_step, c * NWIN + window_count(g, steps))
                pool.wait_ge(corr_reset, c + 1)
                tt_(out=src[:, HALO:2 * HALO], in0=src[:, HALO:2 * HALO], in1=corr[:, g, :],
                    op=ALU.mult).then_inc(window_step, 1)

            def pooled_part(c, g):
                n = POOL_ORDER.index(g)
                pool.wait_ge(pooled_high, c * GROUPS + n + 1)
                tt_(out=pooled_lo[:, :], in0=pooled[:, :], in1=pooled_hi[:, :].bitcast(F32),
                    op=ALU.subtract).then_inc(pooled_split, 1)

            def mix_p_part(c, g):
                n = POOL_ORDER.index(g)
                pool.wait_ge(mix_p_high, c * GROUPS + n + 1)
                tt_(out=mix_lo[:, g, :], in0=mix_p[:, :], in1=mix_hi[:, g, :].bitcast(F32),
                    op=ALU.subtract).then_inc(mix_p_split, 1)

            def unit_band(c, n):
                if n:
                    pool.wait_ge(av_ready, c * NU + n)
                pool.wait_ge(t_high, c * (NU + 1) + n + 2)
                shape = [P, 2, GQ, P]
                mask = masks[:, :, :].unsqueeze(2).broadcast_to(shape)
                tt_(out=band_hi[:, :, :, :], in0=pt_hi[:, :, :].bitcast(F32).unsqueeze(1).broadcast_to(shape),
                    in1=mask, op=ALU.mult).then_inc(band_hi_ready, 1)
                pool.wait_ge(t_low, c * (NU + 1) + n + 2)
                tt_(out=band_lo[:, :, :, :], in0=pt_lo[:, :, :].bitcast(F32).unsqueeze(1).broadcast_to(shape),
                    in1=mask, op=ALU.mult).then_inc(band_lo_ready, 1)

            def unit_mix(c, n):
                b, g = UNITS[n]
                at = (slice(None), slice(4 + 2 * g, 6 + 2 * g), slice(b * P, (b + 1) * P))
                pool.wait_ge(mix_a_high, c * NU + n + 1)
                tt_(out=mix_lo[at], in0=mix_a[:, :, :], in1=mix_hi[at].bitcast(F32),
                    op=ALU.subtract).then_inc(mix_a_split, 1)

            def attention(c, s):
                if s is None:
                    return
                if s in TRANSPOSE_AT:
                    unit_band(c, TRANSPOSE_AT[s])
                if s in MIX_AT:
                    unit_mix(c, MIX_AT[s])

            def chunk(c, last):
                for i in range(NW):
                    if 1 <= i <= NT and TILES[i - 1] in AFTER:
                        mix_p_part(c, int(AFTER[TILES[i - 1]][1]))
                    if i < NT and TILES[i] == "p0":
                        pooled_part(c, 0)
                    attention(c, step_of(i, 0))
                    if i < NT and TILES[i][0] == "u":
                        window_sums(c, int(TILES[i][1]))
                    if i < NT and TILES[i] in ("p3", "p2", "p1"):
                        pooled_part(c, int(TILES[i][1]))
                    attention(c, step_of(i, 1))
                pool.wait_ge(var_ready, c + 1)
                tt_(out=rstd[:, :], in0=var_eps[:, :], in1=minus_half[:, :], op=ALU.pow).then_inc(rstd_ready, 1)

            with pool.Fori(0, CHUNKS - 1) as c:
                chunk(c, False)
            chunk(CHUNKS - 1, True)


def shape_constants():
    import numpy as np

    m = np.arange(BIAS_ROW)
    dist = 2 * P - 1 - m
    valid = (dist >= 0) & (dist < P)
    exact = BUCKETS // 2
    far = np.log(np.maximum(dist, 1).astype(np.float32) / exact) / np.log(P / exact) * (BUCKETS - exact)
    bucket = np.where(dist < exact, dist, np.minimum(exact + far.astype(np.int32), BUCKETS - 1))
    onehot = np.zeros((BUCKETS + 1, BIAS_ROW), np.float32)
    onehot[bucket[valid], m[valid]] = 1.0
    onehot[BUCKETS, ~valid] = NEG_INF
    key, query = np.arange(P)[:, None], np.arange(P)[None, :]
    masks = np.stack([key > query, key <= query], 1).astype(np.float32)
    windows = 2.0 ** np.arange(1, GROUPS + 1)[:, None]
    counts = np.minimum(np.arange(HALO)[None, :] + 1, windows)
    first = np.broadcast_to((windows / counts).astype(np.float32), (P, GROUPS, HALO))
    return onehot, np.eye(P, dtype=np.float32), masks, np.ascontiguousarray(first)


def kernel(x, ln_g, ln_b, w_in, pool_w, pool_scale, sinks, w_out, rel_bias):
    import numpy as np
    import concourse.bacc as bacc
    from concourse.bass_utils import run_bass_kernel_spmd

    x, w_in, w_out = np.asarray(x)[0], np.asarray(w_in)[0], np.asarray(w_out)[0]
    order = {"u": 0, "p": 4, "q": 8, "k": 12, "v": 13, "a": 14}
    tiles = w_in.reshape(KT, P, -1, P).transpose(2, 1, 0, 3)
    tiles = [tiles[order[t[0]] + int(t[1:] or 0)].reshape(P, D) for t in TILES]
    slots = w_out.reshape(KT // 2, 2, P, 2, CH).transpose(3, 0, 2, 1, 4)
    slots = [slots[n, kp].reshape(P, D) for n, kp in SLOTS]
    onehot, identity, masks, first = shape_constants()
    arrays = {
        "x_t": x.reshape(CHUNKS, CH, KT, P).transpose(0, 3, 2, 1),
        "x_rows": x.reshape(CHUNKS, BLOCKS, P, D),
        "weights": np.stack(tiles + slots),
        "pool_w": np.asarray(pool_w)[0].transpose(1, 0, 2),
        "pool_scale": np.asarray(pool_scale)[0].reshape(GROUPS, P).T,
        "sinks": np.broadcast_to(np.asarray(sinks)[0], (P, HEADS)),
        "rel_bias": np.asarray(rel_bias),
        "ln_g": np.broadcast_to(np.asarray(ln_g)[0], (P, D)),
        "ln_b": np.broadcast_to(np.asarray(ln_b)[0], (P, D)),
        "buckets": onehot,
        "identity": identity,
        "band_masks": masks,
        "first_counts": first,
    }
    arrays = {n: np.ascontiguousarray(a) for n, a in arrays.items()}
    nc = bacc.Bacc("TRN2", target_bir_lowering=False, num_devices=1, dynamic_dma_scratch_size=1024)
    args = [nc.dram_tensor(n, a.shape, F32, kind="ExternalInput").ap() for n, a in arrays.items()]
    args.append(nc.dram_tensor("scratch", (HEADS * P * BIAS_ROW,), F32, kind="Internal").ap())
    args.append(nc.dram_tensor("out", (CHUNKS, BLOCKS, P, D), F32, kind="ExternalOutput").ap())
    hybrid_layer(nc, *args)
    r = run_bass_kernel_spmd(nc, [arrays], core_ids=[0])
    return r.results[0]["out"].reshape(1, SEQ, D)
```

```python
import concourse.bass as bass
from concourse import mybir
from contextlib import ExitStack

F32 = mybir.dt.float32
F32R = mybir.dt.float32r
ALU = mybir.AluOpType
ACT = mybir.ActivationFunctionType
AX = mybir.AxisListType

P = 128
D = 1024
SEQ = 2048
CH = 512
CHUNKS = SEQ // CH
KT = D // P
BLOCKS = CH // P
HD = 64
HEADS = 8
KV = 2
GQ = HEADS // KV
GROUPS = 4
HALO = 16
BUCKETS = 32
BIAS_ROW = 3 * P
NEG_INF = -1e30
ALPHA = 2.0 ** 0.25
LN_EPS = 1e-5
SCALE = HD ** -0.5

TILES = ["k", "v", "q0", "q1", "u3", "q2", "q3", "a0", "a1", "a2", "a3",
         "u2", "p3", "u1", "p2", "u0", "p1", "p0"]
NT = len(TILES)
PAIRS = (1, 0, 2, 3)
SLOTS = [(n, kp) for n in range(2) for kp in PAIRS]
NS = len(SLOTS)
NW = NT + NS
AFTER = {"u2": "m3", "u1": "m2", "u0": "m1", "p0": "m0"}
ITEMS = [x for t in TILES for x in ([t, AFTER[t]] if t in AFTER else [t])]
NI = len(ITEMS)
NDONE = NI + NS
POOLED_AT = {"q3": 3, "p3": 2, "p2": 1}
GATES = [x for x in TILES if x[0] in "ap"]
POOL_ORDER = [3, 2, 1, 0]
UNITS = [(b, g) for b in range(BLOCKS) for g in range(KV)]
NU = len(UNITS)
STEP0 = TILES.index("q2")
START = [0, 4, 7, 10, 13, 16, 19, 22]


def at(delay):
    return {s + delay: n for n, s in enumerate(START)}


SCORES_AT, EXP_AT, NORM_AT, TRANSPOSE_AT, VALUES_AT, MIX_AT = at(0), at(1), at(2), at(4), at(7), at(8)
FIRST_TOKENS = (2, 3, 0, 1)
LAST_TOKENS = (FIRST_TOKENS, (0, 1, 2, 3))
HALF1 = NT + NS // 2
IN_PLACE_OF_X = (HALF1, HALF1 + 1)
WARM_UP = 10
WINDOW_STEPS = {3: 4, 2: 3, 1: 2, 0: 1}


def step_of(i, half):
    s = 2 * (i - STEP0) + half
    return s if s >= 0 else None


def done(name):
    return ITEMS.index(name) + 1


def tile_done(i):
    if i >= NW:
        return NDONE + tile_done(i - NW)
    return done(TILES[i]) if i < NT else NI + (i - NT) + 1


def splits_behind(i, last):
    if last and i > NT:
        return {NT + 1: (NT + 3, NT + 4), NT + 2: (NT + 5,), NT + 3: (NT + 6, NT + 7)}.get(i, ())
    return (i + 2,) if 1 <= i < NW - 1 else ()


def window_count(group, k):
    before = POOL_ORDER[:POOL_ORDER.index(group)]
    return sum(WINDOW_STEPS[g] + 1 for g in before) + k


NWIN = sum(WINDOW_STEPS.values()) + GROUPS


def hybrid_layer(nc, x_t, x_rows, weights, pool_w, pool_scale, sinks, rel_bias, ln_g, ln_b,
                 buckets, identity, band_masks, first_counts, scratch, out):
    ctx = ExitStack()
    with ctx:
        def sb(name, shape, dt=F32):
            return ctx.enter_context(nc.sbuf_tensor(name, shape, dt))

        def sem(name):
            return ctx.enter_context(nc.semaphore(name))

        NX = 4
        x_stage = sb("x_stage", [P, NX, CH])
        x_hi = sb("x_hi", [P, KT, CH], F32R)
        x_lo = sb("x_lo", [P, KT, CH], F32R)
        w_stage = sb("w_stage", [P, 2, D])
        w_hi = sb("w_hi", [P, 2, D], F32R)
        w_lo = sb("w_lo", [P, 2, D], F32R)
        pool_w_hi = sb("pool_w_hi", [P, GROUPS, P], F32R)
        pool_w_lo = sb("pool_w_lo", [P, GROUPS, P], F32R)
        q2 = sb("q2", [P, HEADS, CH], F32R)
        k_hi2 = sb("k_hi2", [P, KV, P + CH], F32R)
        k_lo2 = sb("k_lo2", [P, KV, P + CH], F32R)
        v2 = sb("v2", [P, 1 + BLOCKS, KV, P], F32R)
        v_t = sb("v_t", [P, CH])
        tanh_t = sb("tanh_t", [P, 2, CH])
        gate_a = sb("gate_a", [P, 4, CH])
        gate_p = sb("gate_p", [P, CH])
        u_ext = sb("u_ext", [P, GROUPS, HALO + CH])
        win = [sb("win_a", [P, HALO + CH]), sb("win_b", [P, HALO + CH])]
        pooled = sb("pooled", [P, CH])
        pooled_hi = sb("pooled_hi", [P, CH], F32R)
        pooled_lo = sb("pooled_lo", [P, CH], F32R)
        mix_p = sb("mix_p", [P, CH])
        mix_a = sb("mix_a", [P, 2, P])
        mix_hi = sb("mix_hi", [P, KT, CH], F32R)
        mix_lo = sb("mix_lo", [P, KT, CH], F32R)
        bias = sb("bias", [P, HEADS, 2 * P])
        scores = sb("scores", [P, GQ, 2 * P])
        probs = sb("probs", [P, GQ, P])
        pt_hi = sb("pt_hi", [P, GQ, P], F32R)
        pt_lo = sb("pt_lo", [P, GQ, P], F32R)
        band_hi = sb("band_hi", [P, 2, GQ, P], F32R)
        band_lo = sb("band_lo", [P, 2, GQ, P], F32R)
        av_sum = sb("av_sum", [P, 2, P])
        resid = sb("resid", [P, BLOCKS, D])

        def w_parts(i, last):
            if last and i in IN_PLACE_OF_X:
                k = 2 * IN_PLACE_OF_X.index(i)
                return [x[:, k:k + 2, :].rearrange("p k t -> p (k t)") for x in (x_hi, x_lo)]
            return w_hi[:, i % 2, :], w_lo[:, i % 2, :]

        def first_x(k):
            return x_stage[:, k, :] if k < NX else resid[:, k - NX, 0:CH]

        ln_g_sb = sb("ln_g_sb", [P, D])
        ln_b_sb = sb("ln_b_sb", [P, D])
        ident = sb("ident", [P, P])
        masks = sb("masks", [P, 2, P])
        corr = sb("corr", [P, GROUPS, HALO])
        sinks_sb = sb("sinks_sb", [P, HEADS])
        neg_sinks = sb("neg_sinks", [P, HEADS])
        scale_sb = sb("scale_sb", [P, GROUPS])
        half_scale = sb("half_scale", [P, GROUPS])
        rel_ext = sb("rel_ext", [BUCKETS + 1, HEADS])
        onehot = pooled[0:BUCKETS + 1, 0:BIAS_ROW]
        bias_row = mix_p[0:HEADS, 0:BIAS_ROW]
        prev_mask = sb("prev_mask", [P, 1])
        row_max = sb("row_max", [P, GQ])
        neg_max = sb("neg_max", [P, GQ])
        sink_shift = sb("sink_shift", [P, GQ])
        sink_exp = sb("sink_exp", [P, GQ])
        exp_sum = sb("exp_sum", [P, GQ])
        total = sb("total", [P, GQ])
        inv_total = sb("inv_total", [P, GQ])
        stats = sb("stats", [P, BLOCKS, 2, 6])
        mean_var = sb("mean_var", [P, BLOCKS, 2])
        var_eps = sb("var_eps", [P, BLOCKS])
        minus_half = sb("minus_half", [P, BLOCKS])
        rstd = sb("rstd", [P, BLOCKS])

        acc = [ctx.enter_context(nc.psum_tensor(f"acc{i}", [P, CH], F32)) for i in range(4)]
        s_ps = ctx.enter_context(nc.psum_tensor("s_ps", [P, GQ, 2 * P], F32))
        t_ps = ctx.enter_context(nc.psum_tensor("t_ps", [P, GQ, P], F32))
        v_ps = ctx.enter_context(nc.psum_tensor("v_ps", [P, GQ, P], F32))

        consts_loaded = sem("consts_loaded")
        tables_loaded = sem("tables_loaded")
        ln_loaded = sem("ln_loaded")
        keys_cleared = sem("keys_cleared")
        cleared = sem("cleared")
        ext_ready = sem("ext_ready")
        row_ready = sem("row_ready")
        row_copied = sem("row_copied")
        row_stored = sem("row_stored")
        bias_loaded = sem("bias_loaded")
        derived = sem("derived")
        pool_w_high = sem("pool_w_high")
        pool_w_split = sem("pool_w_split")
        w_loaded = [sem("w_loaded0"), sem("w_loaded1")]
        w_high = sem("w_high")
        w_split = sem("w_split")
        x_loaded = [sem(f"x_loaded{i}") for i in range(NX)]
        first_x_loaded = [sem(f"first_x_loaded{k}") for k in range(KT)]
        x_high = sem("x_high")
        x_split = sem("x_split")
        pe_done = sem("pe_done")
        hi_ready = sem("hi_ready")
        low_ready = sem("low_ready")
        gate_ready = sem("gate_ready")
        scores_ready = sem("scores_ready")
        biased = sem("biased")
        first_masked = sem("first_masked")
        merged = sem("merged")
        max_ready = sem("max_ready")
        neg_max_ready = sem("neg_max_ready")
        shift_ready = sem("shift_ready")
        exp_ready = sem("exp_ready")
        total_ready = sem("total_ready")
        inv_ready = sem("inv_ready")
        probs_ready = sem("probs_ready")
        halo_k = sem("halo_k")
        halo_k_low = sem("halo_k_low")
        halo_v = sem("halo_v")
        t_ready = sem("t_ready")
        t_high = sem("t_high")
        t_low = sem("t_low")
        band_hi_ready = sem("band_hi_ready")
        band_lo_ready = sem("band_lo_ready")
        av_ready = sem("av_ready")
        av_copied = sem("av_copied")
        av_summed = sem("av_summed")
        mix_a_ready = sem("mix_a_ready")
        mix_a_high = sem("mix_a_high")
        mix_a_split = sem("mix_a_split")
        window_step = sem("window_step")
        pooled_ready = sem("pooled_ready")
        halo_u = sem("halo_u")
        pooled_high = sem("pooled_high")
        pooled_split = sem("pooled_split")
        mix_p_ready = sem("mix_p_ready")
        mix_p_high = sem("mix_p_high")
        mix_p_split = sem("mix_p_split")
        corr_reset = sem("corr_reset")
        mask_reset = sem("mask_reset")
        resid_loaded = [sem(f"resid_loaded{i}") for i in range(BLOCKS)]
        out_part = sem("out_part")
        sum_ready = sem("sum_ready")
        stats_ready = sem("stats_ready")
        stats_seen = sem("stats_seen")
        aggr_ready = sem("aggr_ready")
        var_ready = sem("var_ready")
        rstd_ready = sem("rstd_ready")
        centred = sem("centred")
        scaled = sem("scaled")
        ln_done = [sem(f"ln_done{i}") for i in range(BLOCKS)]
        out_stored = [sem(f"out_stored{i}") for i in range(BLOCKS)]

        block = ctx.enter_context(nc.Block())
        NCONST, TABLES = 3, 6

        @block.sync
        def _(sp):
            def load_w(i):
                sp.dma_start(w_stage[:, i % 2, :], weights[i % NW]).then_inc(w_loaded[i % 2], 16)

            def load_x(c, k):
                sp.dma_start(x_stage[:, k % NX, :], x_t[c, :, k, :]).then_inc(x_loaded[k % NX], 16)

            def load_first_x(k):
                sp.dma_start(first_x(k), x_t[0, :, k, :]).then_inc(first_x_loaded[k], 16)

            def load_rows(c, tt):
                sp.dma_start(resid[:, tt, :], x_rows[c, tt]).then_inc(resid_loaded[tt], 16)

            HEAD = 12
            STORE_AT = {3: (0, 1), 4: (2,), 5: (3,)}
            LOAD_AT = {7: 0, 8: 1, 9: 2, 10: 3}

            def stream(c, tiles, last=False):
                for i in tiles:
                    if not (last and i + 2 >= NW):
                        sp.wait_ge(w_split, c * NW + i + 1)
                        load_w(i + 2)
                    if not last and NT - 6 <= i < NT - 2:
                        load_x(c + 1, i - (NT - 6))
                    if not last and NT + 2 <= i < NT + 2 + KT - NX:
                        k = i - NT - 2 + NX
                        sp.wait_ge(x_split, c * KT + KT + k - NX + 1)
                        load_x(c + 1, k)

            def store_rows(c, tt):
                sp.wait_ge(ln_done[tt], c + 1)
                sp.dma_start(out[c, tt], resid[:, tt, :]).then_inc(out_stored[tt], 16)

            def head(c):
                for i in range(HEAD):
                    stream(c + 1, [i])
                    for tt in STORE_AT.get(i, ()):
                        store_rows(c, tt)
                    if i in LOAD_AT:
                        tt = LOAD_AT[i]
                        sp.wait_ge(out_stored[tt], (c + 1) * 16)
                        load_rows(c + 1, tt)

            load_first_x(0)
            load_w(0)
            for k in range(1, KT):
                load_first_x(k)
            load_w(1)
            stream(0, range(2))

            sp.wait_ge(row_copied, 1)
            sp.dma_start(scratch.rearrange("(h i m) -> h i m", h=HEADS, i=P),
                         bias_row.unsqueeze(1).broadcast_to([HEADS, P, BIAS_ROW])).then_inc(row_stored, 16)
            stream(0, range(2, 4))
            sp.wait_ge(row_stored, 16)
            for h in range(HEADS):
                at = h * P * BIAS_ROW + P - 1
                skewed = scratch[at:at + P * (BIAS_ROW - 1)].rearrange("(i m) -> i m", i=P)
                sp.dma_start(bias[:, h, :], skewed[:, 0:2 * P]).then_inc(bias_loaded, 16)

            stream(0, range(4, 6))
            sp.dma_start(ln_g_sb[:, :], ln_g).then_inc(ln_loaded, 16)
            sp.dma_start(ln_b_sb[:, :], ln_b).then_inc(ln_loaded, 16)
            sp.wait_ge(x_split, KT)
            for tt in range(BLOCKS):
                load_rows(0, tt)
            stream(0, range(6, HEAD))
            with sp.Fori(0, CHUNKS - 1) as c:
                stream(c, range(HEAD, NW))
                head(c)
            stream(CHUNKS - 1, range(HEAD, NW), True)
            for tt in range(BLOCKS - 1):
                store_rows(CHUNKS - 1, tt)
            tt = BLOCKS - 1
            for h in range(2):
                sp.wait_ge(ln_done[tt], CHUNKS + h)
                cols = slice(h * CH, (h + 1) * CH)
                sp.dma_start(out[CHUNKS - 1, tt][:, cols], resid[:, tt, cols]).then_inc(out_stored[tt], 16)
            for tt in range(BLOCKS):
                halves = 2 if tt == BLOCKS - 1 else 1
                sp.wait_ge(out_stored[tt], (CHUNKS - 1 + halves) * 16)

        @block.tensor
        def _(pe):
            mm = nc.tensor.matmul

            pe.wait_ge(keys_cleared, 1)
            for _ in range(WARM_UP):
                mm(t_ps[:, :, :], k_hi2[:, 0, 0:P], k_hi2[:, 0, 0:CH], start=True, stop=True)

            pe.wait_ge(consts_loaded, NCONST * 16)
            pe.wait_ge(ext_ready, 1)
            mm(v_ps[0:HEADS, 0:3, :], rel_ext[:, :], onehot, start=True, stop=True).then_inc(row_ready, 1)

            def bank_free(c, idx):
                if idx < 4:
                    pe.wait_ge(sum_ready, c * 2 * BLOCKS + BLOCKS + idx + 1)
                    return
                name = ITEMS[idx - 4] if idx < NI + 4 else None
                kind = name[0]
                if kind in "kq":
                    n = 0 if kind == "k" else 1 + int(name[1])
                    pe.wait_ge(low_ready, c * 5 + n + 1)
                elif kind in "vu":
                    pe.wait_ge(hi_ready, c * NT + TILES.index(name) + 1)
                elif kind in "ap":
                    pe.wait_ge(gate_ready, c * 8 + GATES.index(name) + 1)
                else:
                    pe.wait_ge(mix_p_ready, c * GROUPS + POOL_ORDER.index(int(name[1])) + 1)

            def tile_half(c, i, half):
                idx = ITEMS.index(TILES[i])
                w, to = i % 2, acc[idx % 4][:, :]
                if half == 0:
                    bank_free(c, idx)
                    pe.wait_ge(w_split, c * NW + i + 1)
                for k in range(4 * half, 4 * half + 4):
                    if i == 0:
                        pe.wait_ge(x_split, c * KT + k + 1)
                    cols = slice(k * P, (k + 1) * P)
                    mm(to, w_hi[:, w, cols], x_hi[:, k, :], start=(k == 0), stop=False)
                    mm(to, w_hi[:, w, cols], x_lo[:, k, :], start=False, stop=False)
                    last = mm(to, w_lo[:, w, cols], x_hi[:, k, :], start=False, stop=(k == KT - 1))
                if half == 1:
                    last.then_inc(pe_done, 1)

            def pool_product(c, name):
                g = int(name[1])
                idx = ITEMS.index(name)
                to = acc[idx % 4][:, :]
                bank_free(c, idx)
                pe.wait_ge(pooled_split, c * GROUPS + POOL_ORDER.index(g) + 1)
                if g == POOL_ORDER[0]:
                    pe.wait_ge(pool_w_split, 1)
                mm(to, pool_w_hi[:, g, :], pooled_hi[:, :], start=True, stop=False)
                mm(to, pool_w_hi[:, g, :], pooled_lo[:, :], start=False, stop=False)
                mm(to, pool_w_lo[:, g, :], pooled_hi[:, :], start=False, stop=True).then_inc(pe_done, 1)

            def transpose_values(c):
                pe.wait_ge(hi_ready, c * NT + 2)
                for b in range(BLOCKS):
                    last = nc.tensor.transpose(t_ps[:, b, :], v_t[:, b * P:(b + 1) * P], ident[:, :])
                last.then_inc(t_ready, 1)

            def unit_scores(c, n):
                b, g = UNITS[n]
                if b == 0:
                    pe.wait_ge(low_ready, c * 5 + 3 + 2 * g)
                if n:
                    pe.wait_ge(biased, c * NU + n)
                for h in range(GQ):
                    to = s_ps[:, h, :]
                    q = q2[:, g * GQ + h, b * P:(b + 1) * P]
                    mm(to, q, k_hi2[:, g, b * P:b * P + 2 * P], start=True, stop=False)
                    last = mm(to, q, k_lo2[:, g, b * P:b * P + 2 * P], start=False, stop=True)
                last.then_inc(scores_ready, 1)

            def unit_transpose(c, n):
                pe.wait_ge(probs_ready, c * NU + n + 1)
                pe.wait_ge(t_low, c * (NU + 1) + n + 1)
                for h in range(GQ):
                    last = nc.tensor.transpose(t_ps[:, h, :], probs[:, h, :], ident[:, :])
                last.then_inc(t_ready, 1)

            def unit_values(c, n):
                b, g = UNITS[n]
                pe.wait_ge(band_hi_ready, c * NU + n + 1)
                pe.wait_ge(band_lo_ready, c * NU + n + 1)
                if n:
                    pe.wait_ge(av_summed, c * NU + n)
                for j in range(2):
                    v = v2[:, b + j, g, :]
                    mm(v_ps[:, :, :], v, band_hi[:, j, :, :], start=(j == 0), stop=False)
                    last = mm(v_ps[:, :, :], v, band_lo[:, j, :, :], start=False, stop=(j == 1))
                last.then_inc(av_ready, 1)

            def out_half(c, s, half):
                n, kp = SLOTS[s]
                i = NT + s
                if half == 0:
                    pe.wait_ge(w_split, c * NW + i + 1)
                if kp < 2:
                    g = 2 * kp if kp == PAIRS[0] else 2 * kp + 1 - half
                    pe.wait_ge(mix_p_split, c * GROUPS + POOL_ORDER.index(g) + 1)
                else:
                    if half == 0:
                        pe.wait_ge(mix_a_split, c * NU + NU - (kp == 2))
                if kp in (PAIRS[0], PAIRS[-1]):
                    tokens = FIRST_TOKENS if kp == PAIRS[0] else LAST_TOKENS[n]
                    order = [(tt, h) for tt in tokens[2 * half:2 * half + 2] for h in range(2)]
                else:
                    h = 1 - half if kp < 2 else half
                    order = [(tt, h) for tt in range(BLOCKS)]
                last = out_products(c, s, order, False)
                if half == 1:
                    last.then_inc(pe_done, 1)

            def out_products(c, s, order, last):
                n, kp = SLOTS[s]
                high, low = w_parts(NT + s, last)
                for tt, h in order:
                    k = 2 * kp + h
                    first = kp == PAIRS[0] and h == 0
                    final = kp == PAIRS[-1] and h == 1
                    if first and n == 0:
                        bank_free_out(c, tt)
                    if first and n == 1:
                        pe.wait_ge(sum_ready, c * 2 * BLOCKS + 2 * BLOCKS + LAST_TOKENS[0].index(tt) + 1)
                    to = acc[tt][:, :]
                    rows = slice(tt * P, (tt + 1) * P)
                    cols = slice(h * CH, (h + 1) * CH)
                    mm(to, mix_hi[:, k, rows], high[:, cols], start=first, stop=False)
                    mm(to, mix_hi[:, k, rows], low[:, cols], start=False, stop=False)
                    product = mm(to, mix_lo[:, k, rows], high[:, cols], start=False, stop=final)
                    if final and tt != LAST_TOKENS[n][-1]:
                        product.then_inc(out_part, 1)
                return product

            def out_end(c):
                for tt in LAST_TOKENS[1]:
                    for s in range(NS // 2, NS):
                        if tt == LAST_TOKENS[1][0]:
                            pe.wait_ge(w_split, c * NW + NT + s + 1)
                        last = out_products(c, s, [(tt, h) for h in range(2)], True)
                        if tt == LAST_TOKENS[1][-1]:
                            last.then_inc(pe_done, 1)

            def bank_free_out(c, tt):
                idx = max(j for j in range(NI) if j % 4 == tt)
                bank_free(c, idx + 4)

            def attention(c, s):
                if s is None:
                    return
                if s in TRANSPOSE_AT:
                    unit_transpose(c, TRANSPOSE_AT[s])
                if s in SCORES_AT:
                    unit_scores(c, SCORES_AT[s])
                if s in VALUES_AT:
                    unit_values(c, VALUES_AT[s])

            def chunk(c, last):
                for i in range(HALF1 if last else NW):
                    for half in range(2):
                        if i < NT:
                            tile_half(c, i, half)
                        else:
                            out_half(c, i - NT, half)
                        attention(c, step_of(i, half))
                        if (i, half) == (3, 0):
                            transpose_values(c)
                    if i < NT and TILES[i] in AFTER:
                        pool_product(c, AFTER[TILES[i]])
                if last:
                    out_end(c)

            with pe.Fori(0, CHUNKS - 1) as c:
                chunk(c, False)
            chunk(CHUNKS - 1, True)

        @block.scalar
        def _(act):
            copy = lambda o, i: nc.scalar.activation(o, i, ACT.Copy)

            for o, i in ((rel_ext[0:BUCKETS, :], rel_bias), (onehot, buckets), (ident[:, :], identity)):
                act.dma_start(o, i).then_inc(consts_loaded, 16)

            def split_w(c, i, last=False):
                if last and i in IN_PLACE_OF_X:
                    act.wait_ge(pe_done, c * NDONE + NI)
                elif last and i > HALF1:
                    act.wait_ge(pe_done, c * NDONE + tile_done(i - 4))
                elif i >= 2:
                    act.wait_ge(pe_done, c * NDONE + tile_done(i - 2))
                act.wait_ge(w_loaded[i % 2], (c * (NW // 2) + i // 2 + 1) * 16)
                copy(w_parts(i, last)[0], w_stage[:, i % 2, :]).then_inc(w_high, 1)

            def split_x(c, k):
                act.wait_ge(x_loaded[k % NX], ((c - 1) * (KT // NX) + k // NX + 1) * 16)
                copy(x_hi[:, k, :], x_stage[:, k % NX, :]).then_inc(x_high, 1)

            def split_first_x(k):
                act.wait_ge(first_x_loaded[k], 16)
                copy(x_hi[:, k, :], first_x(k)).then_inc(x_high, 1)

            split_first_x(0)
            split_w(0, 0)
            for k in range(1, KT):
                split_first_x(k)
            split_w(0, 1)
            act.wait_ge(row_ready, 1)
            copy(bias_row, v_ps[0:HEADS, 0:3, :].rearrange("h a m -> h (a m)")).then_inc(row_copied, 1)
            for o, i in ((sinks_sb[:, :], sinks), (scale_sb[:, :], pool_scale), (masks[:, :, :], band_masks),
                         (corr[:, :, :], first_counts), (mix_a[:, :, :], pool_w[:, 0:2, :]),
                         (av_sum[:, :, :], pool_w[:, 2:4, :])):
                act.dma_start(o, i).then_inc(tables_loaded, 16)
            split_w(0, 2)
            act.wait_ge(tables_loaded, TABLES * 16)
            copy(pool_w_hi[:, 0:2, :], mix_a[:, :, :])
            copy(pool_w_hi[:, 2:4, :], av_sum[:, :, :]).then_inc(pool_w_high, 1)
            act.wait_ge(cleared, 1)

            def evacuate(c, i):
                name = TILES[i]
                kind, t = name[0], int(name[1:] or 0)
                act.wait_ge(pe_done, c * NDONE + done(name))
                src = acc[ITEMS.index(name) % 4]
                if kind == "k":
                    copy(k_hi2[:, :, 0:P], k_hi2[:, :, CH:CH + P].bitcast(F32)).then_inc(halo_k, 1)
                    act.wait_ge(halo_k, c + 1)
                    for a in range(KV):
                        for r in range(2):
                            last = copy(k_hi2[r * HD:(r + 1) * HD, a, P:], src[a * HD:(a + 1) * HD, :])
                elif kind == "v":
                    last = copy(v_t[:, :], src[:, :])
                elif kind == "q":
                    for a in range(2):
                        last = copy(q2[0:HD, 2 * t + a, :], src[a * HD:(a + 1) * HD, :])
                elif kind == "u":
                    copy(u_ext[:, t, 0:HALO], u_ext[:, t, CH:CH + HALO]).then_inc(halo_u, 1)
                    act.wait_ge(halo_u, c * GROUPS + POOL_ORDER.index(t) + 1)
                    last = copy(u_ext[:, t, HALO:], src[:, :])
                else:
                    m = GATES.index(name)
                    if m >= 2:
                        act.wait_ge(gate_ready, c * 8 + m - 1)
                    last = nc.scalar.activation(tanh_t[:, m % 2, :], src[:, :], ACT.Tanh, scale=0.5)
                last.then_inc(hi_ready, 1)

            def split_values(c):
                act.wait_ge(t_ready, c * (NU + 1) + 1)
                copy(v2[:, 0, :, :], v2[:, BLOCKS, :, :].bitcast(F32)).then_inc(halo_v, 1)
                act.wait_ge(halo_v, c + 1)
                copy(v2[:, 1:, :, 0:HD], t_ps[:, :, :].rearrange("p b (g d) -> p b g d", g=KV)).then_inc(t_high, 1)

            def unit_exp(c, n):
                act.wait_ge(shift_ready, c * NU + n + 1)
                if n:
                    act.wait_ge(total_ready, c * NU + n)
                act.wait_ge(t_ready, c * (NU + 1) + n + 1)
                nc.scalar.activation(sink_exp[:, :], sink_shift[:, :], ACT.Exp)
                for h in range(GQ):
                    last = nc.scalar.activation(probs[:, h, :], scores[:, h, 0:P], ACT.Exp,
                                                bias=neg_max[:, h:h + 1], accum_out=exp_sum[:, h:h + 1])
                last.then_inc(exp_ready, 1)

            def unit_pt_high(c, n):
                act.wait_ge(t_ready, c * (NU + 1) + n + 2)
                if n:
                    act.wait_ge(band_hi_ready, c * NU + n)
                copy(pt_hi[:, :, :], t_ps[:, :, :]).then_inc(t_high, 1)

            def unit_av_copy(c, n):
                act.wait_ge(av_ready, c * NU + n + 1)
                copy(v_t[0:HD, :], v_ps[HD:P, :, :].rearrange("p h q -> p (h q)")).then_inc(av_copied, 1)

            def unit_mix(c, n):
                b, g = UNITS[n]
                act.wait_ge(mix_a_ready, c * NU + n + 1)
                copy(mix_hi[:, 4 + 2 * g:6 + 2 * g, b * P:(b + 1) * P], mix_a[:, :, :]).then_inc(mix_a_high, 1)

            def pooled_part(c, g):
                n = POOL_ORDER.index(g)
                act.wait_ge(pooled_ready, c * GROUPS + n + 1)
                if n:
                    act.wait_ge(pe_done, c * NDONE + done(f"m{POOL_ORDER[n - 1]}"))
                copy(pooled_hi[:, :], pooled[:, :]).then_inc(pooled_high, 1)

            def mix_p_part(c, g):
                n = POOL_ORDER.index(g)
                act.wait_ge(mix_p_ready, c * GROUPS + n + 1)
                copy(mix_hi[:, g, :], mix_p[:, :]).then_inc(mix_p_high, 1)

            def attention(c, s):
                if s is None:
                    return
                if s in TRANSPOSE_AT:
                    unit_pt_high(c, TRANSPOSE_AT[s])
                if s in VALUES_AT:
                    unit_av_copy(c, VALUES_AT[s])
                if s in EXP_AT:
                    unit_exp(c, EXP_AT[s])
                if s in MIX_AT:
                    unit_mix(c, MIX_AT[s])

            def chunk(c, last):
                for i in range(NW):
                    name = TILES[i] if i < NT else None
                    attention(c, step_of(i, 0))
                    if name in ("q0", "q1"):
                        split_w(c, i + 2)
                    if 1 <= i < NT:
                        evacuate(c, i)
                    if name not in ("q0", "q1"):
                        for w in splits_behind(i, last):
                            split_w(c, w, last)
                    if i == 1:
                        evacuate(c, 0)
                    if name == "p1":
                        pooled_part(c, 0)
                    if name and name[0] == "p":
                        mix_p_part(c, int(name[1]))
                    attention(c, step_of(i, 1))
                    if name in POOLED_AT:
                        pooled_part(c, POOLED_AT[name])
                    if i == 3:
                        split_values(c)
                    if not last and i >= NT:
                        if i == NT:
                            act.wait_ge(pe_done, c * NDONE + NI)
                        split_x(c + 1, i - NT)
                if not last:
                    split_w(c, NW + 1)
                for tt in range(BLOCKS - 1 if last else BLOCKS):
                    if tt == 0 and not last:
                        split_w(c, NW + 2)
                    act.wait_ge(rstd_ready, c * BLOCKS + tt + 1)
                    act.wait_ge(centred, c * BLOCKS + tt + 1)
                    nc.scalar.activation(resid[:, tt, :], resid[:, tt, :], ACT.Copy, scale=rstd[:, tt:tt + 1]).then_inc(scaled, 1)

            with act.Fori(0, CHUNKS - 1) as c:
                chunk(c, False)
            chunk(CHUNKS - 1, True)

        @block.vector
        def _(dve):
            tt_ = nc.vector.tensor_tensor
            stt = nc.vector.scalar_tensor_tensor

            dve.sem_inc(sum_ready, 2 * BLOCKS)
            dve.sem_inc(corr_reset, 1)
            nc.vector.memset(prev_mask[:, :], NEG_INF).then_inc(mask_reset, 1)
            nc.vector.memset(rel_ext[BUCKETS:BUCKETS + 1, :], 1.0).then_inc(ext_ready, 1)

            def split_x(k):
                dve.wait_ge(x_high, k + 1)
                tt_(out=x_lo[:, k, :], in0=first_x(k), in1=x_hi[:, k, :].bitcast(F32),
                    op=ALU.subtract).then_inc(x_split, 1)

            def split_w(c, i, last=False):
                high, low = w_parts(i, last)
                dve.wait_ge(w_high, c * NW + i + 1)
                tt_(out=low, in0=w_stage[:, i % 2, :], in1=high.bitcast(F32),
                    op=ALU.subtract).then_inc(w_split, 1)

            split_x(0)
            split_w(0, 0)
            for k in range(1, KT):
                split_x(k)
            split_w(0, 1)
            split_w(0, 2)
            dve.wait_ge(pool_w_high, 1)
            tt_(out=pool_w_lo[:, 0:2, :], in0=mix_a[:, :, :], in1=pool_w_hi[:, 0:2, :].bitcast(F32), op=ALU.subtract)
            tt_(out=pool_w_lo[:, 2:4, :], in0=av_sum[:, :, :], in1=pool_w_hi[:, 2:4, :].bitcast(F32),
                op=ALU.subtract).then_inc(pool_w_split, 1)
            nc.vector.tensor_scalar(neg_sinks[:, :], sinks_sb[:, :], -1.0, None, ALU.mult).then_inc(derived, 1)
            nc.vector.tensor_scalar(half_scale[:, :], scale_sb[:, :], 0.5, None, ALU.mult).then_inc(derived, 1)
            dve.wait_ge(derived, 2)
            dve.wait_ge(cleared, 1)

            def evacuate(c, i):
                name = TILES[i]
                kind, t = name[0], int(name[1:] or 0)
                src = acc[ITEMS.index(name) % 4]
                if kind in "vu":
                    return
                dve.wait_ge(hi_ready, c * NT + max(i, 1) + 1)
                if kind == "k":
                    nc.vector.tensor_copy(k_lo2[:, :, 0:P], k_lo2[:, :, CH:CH + P].bitcast(F32)).then_inc(halo_k_low, 1)
                    dve.wait_ge(halo_k_low, c + 1)
                    for a in range(KV):
                        for r in range(2):
                            rows = slice(r * HD, (r + 1) * HD)
                            last = tt_(out=k_lo2[rows, a, P:], in0=src[a * HD:(a + 1) * HD, :],
                                       in1=k_hi2[rows, a, P:].bitcast(F32), op=ALU.subtract)
                    last.then_inc(low_ready, 1)
                elif kind == "q":
                    for a in range(2):
                        last = tt_(out=q2[HD:P, 2 * t + a, :], in0=src[a * HD:(a + 1) * HD, :],
                                   in1=q2[0:HD, 2 * t + a, :].bitcast(F32), op=ALU.subtract)
                    last.then_inc(low_ready, 1)
                else:
                    m = GATES.index(name)
                    to = gate_a[:, t, :] if kind == "a" else gate_p[:, :]
                    stt(out=to, in0=tanh_t[:, m % 2, :], scalar=1.0, in1=src[:, :],
                        op0=ALU.add, op1=ALU.mult).then_inc(gate_ready, 1)

            def split_values(c):
                dve.wait_ge(t_high, c * (NU + 1) + 1)
                tt_(out=v2[:, 1:, :, HD:P], in0=t_ps[:, :, :].rearrange("p b (g d) -> p b g d", g=KV),
                    in1=v2[:, 1:, :, 0:HD].bitcast(F32), op=ALU.subtract).then_inc(t_low, 1)

            def unit_max(c, n):
                b, g = UNITS[n]
                heads = slice(g * GQ, (g + 1) * GQ)
                dve.wait_ge(scores_ready, c * NU + n + 1)
                if n == 0:
                    dve.wait_ge(bias_loaded, HEADS * 16)
                stt(out=scores[:, :, :], in0=s_ps[:, :, :], scalar=SCALE, in1=bias[:, heads, :],
                    op0=ALU.mult, op1=ALU.add).then_inc(biased, 1)
                dve.wait_ge(biased, c * NU + n + 1)
                if b == 0:
                    dve.wait_ge(mask_reset, c + 1)
                    nc.vector.tensor_scalar(scores[:, :, 0:P], scores[:, :, 0:P], prev_mask[:, 0:1], None,
                                            ALU.add).then_inc(first_masked, 1)
                    dve.wait_ge(first_masked, c * KV + g + 1)
                tt_(out=scores[:, :, 0:P], in0=scores[:, :, 0:P], in1=scores[:, :, P:], op=ALU.max).then_inc(merged, 1)
                dve.wait_ge(merged, c * NU + n + 1)
                nc.vector.tensor_reduce(out=row_max[:, :], in_=scores[:, :, 0:P], op=ALU.max, axis=AX.X).then_inc(max_ready, 1)
                dve.wait_ge(max_ready, c * NU + n + 1)
                stt(out=neg_max[:, :], in0=row_max[:, :], scalar=-1.0, in1=neg_sinks[:, heads],
                    op0=ALU.mult, op1=ALU.min).then_inc(neg_max_ready, 1)
                dve.wait_ge(neg_max_ready, c * NU + n + 1)
                tt_(out=sink_shift[:, :], in0=sinks_sb[:, heads], in1=neg_max[:, :], op=ALU.add).then_inc(shift_ready, 1)

            def unit_normalise(c, n):
                dve.wait_ge(exp_ready, c * NU + n + 1)
                tt_(out=total[:, :], in0=exp_sum[:, :], in1=sink_exp[:, :], op=ALU.add).then_inc(total_ready, 1)
                dve.wait_ge(total_ready, c * NU + n + 1)
                nc.vector.reciprocal(inv_total[:, :], total[:, :]).then_inc(inv_ready, 1)
                dve.wait_ge(inv_ready, c * NU + n + 1)
                tt_(out=probs[:, :, :], in0=probs[:, :, :],
                    in1=inv_total[:, :].unsqueeze(2).broadcast_to([P, GQ, P]), op=ALU.mult).then_inc(probs_ready, 1)

            def unit_pt_low(c, n):
                dve.wait_ge(t_high, c * (NU + 1) + n + 2)
                if n:
                    dve.wait_ge(band_lo_ready, c * NU + n)
                tt_(out=pt_lo[:, :, :], in0=t_ps[:, :, :], in1=pt_hi[:, :, :].bitcast(F32),
                    op=ALU.subtract).then_inc(t_low, 1)

            def unit_gate(c, n):
                b, g = UNITS[n]
                dve.wait_ge(av_copied, c * NU + n + 1)
                low = v_t[0:HD, :].rearrange("p (t a q) -> p t a q", t=2, a=2)
                high = v_ps[0:HD, :, :].rearrange("p (t a) q -> p t a q", a=2)
                for a in range(2):
                    last = tt_(out=av_sum[a * HD:(a + 1) * HD, :, :], in0=high[:, :, a, :], in1=low[:, :, a, :], op=ALU.add)
                last.then_inc(av_summed, 1)
                dve.wait_ge(av_summed, c * NU + n + 1)
                if b == 0:
                    dve.wait_ge(gate_ready, c * 8 + 2 * g + 2)
                if n:
                    dve.wait_ge(mix_a_split, c * NU + n)
                stt(out=mix_a[:, :, :], in0=av_sum[:, :, :], scalar=0.5,
                    in1=gate_a[:, 2 * g:2 * g + 2, b * P:(b + 1) * P], op0=ALU.mult, op1=ALU.mult).then_inc(mix_a_ready, 1)

            def pooled_diff(c, g):
                n = POOL_ORDER.index(g)
                dve.wait_ge(window_step, c * NWIN + window_count(g, WINDOW_STEPS[g] + 1))
                if n:
                    dve.wait_ge(pooled_split, c * GROUPS + n)
                w = win[(WINDOW_STEPS[g] + 1) % 2]
                stt(out=pooled[:, :], in0=w[:, HALO:], scalar=1.0 / 2 ** (g + 1), in1=u_ext[:, g, HALO:],
                    op0=ALU.mult, op1=ALU.subtract).then_inc(pooled_ready, 1)

            def mix_p_gate(c, g):
                n = POOL_ORDER.index(g)
                dve.wait_ge(pe_done, c * NDONE + done(f"m{g}"))
                dve.wait_ge(gate_ready, c * 8 + GATES.index(f"p{g}") + 1)
                if n:
                    dve.wait_ge(mix_p_split, c * GROUPS + n)
                src = acc[ITEMS.index(f"m{g}") % 4]
                stt(out=mix_p[:, :], in0=src[:, :], scalar=half_scale[:, g:g + 1], in1=gate_p[:, :],
                    op0=ALU.mult, op1=ALU.mult).then_inc(mix_p_ready, 1)

            def residual(c, n, tt):
                at = LAST_TOKENS[n].index(tt)
                if at < BLOCKS - 1:
                    dve.wait_ge(out_part, c * 6 + n * 3 + at + 1)
                else:
                    dve.wait_ge(pe_done, c * NDONE + NI + 4 * n + 4)
                if n == 0:
                    dve.wait_ge(resid_loaded[tt], (c + 1) * 16)
                part = resid[:, tt, n * CH:(n + 1) * CH]
                stt(out=part, in0=part, scalar=ALPHA, in1=acc[tt][:, :], op0=ALU.mult, op1=ALU.add).then_inc(sum_ready, 1)

            def statistics(c, n, tt):
                at = LAST_TOKENS[n].index(tt)
                dve.wait_ge(sum_ready, c * 2 * BLOCKS + 2 * BLOCKS + n * BLOCKS + at + 1)
                nc.vector.bn_stats(out=stats[:, tt, n, :], in_=resid[:, tt, n * CH:(n + 1) * CH]).then_inc(stats_ready, 1)

            def first_half_sums(c, last):
                t = LAST_TOKENS[0]
                residual(c, 0, t[0])
                statistics(c, 0, t[0])
                residual(c, 0, t[1])
                residual(c, 0, t[2])
                if last:
                    split_w(c, NT + 6, last)
                residual(c, 0, t[3])
                split_w(c, NT + 7 if last else NT + 5, last)
                for tt in t[1:]:
                    statistics(c, 0, tt)

            def norm_scalars(c, tt):
                dve.wait_ge(stats_ready, c * 2 * BLOCKS + BLOCKS + tt + 1)
                dve.sem_inc(stats_seen, 1)
                nc.vector.bn_aggr(out=mean_var[:, tt, :], in_=stats[:, tt, :, :]).then_inc(aggr_ready, 1)
                dve.wait_ge(aggr_ready, c * BLOCKS + tt + 1)
                nc.vector.tensor_scalar(var_eps[:, tt:tt + 1], mean_var[:, tt, 1:2], LN_EPS, None,
                                        ALU.add).then_inc(var_ready, 1)

            def centre(c, tt, cols=slice(0, D)):
                if tt == 0:
                    dve.wait_ge(ln_loaded, 2 * 16)
                stt(out=resid[:, tt, cols], in0=resid[:, tt, cols], scalar=mean_var[:, tt, 0:1], in1=ln_g_sb[:, cols],
                    op0=ALU.subtract, op1=ALU.mult).then_inc(centred, 1)

            def attention(c, s):
                if s is None:
                    return
                if s in NORM_AT:
                    unit_normalise(c, NORM_AT[s])
                if s in TRANSPOSE_AT:
                    unit_pt_low(c, TRANSPOSE_AT[s])
                if s in SCORES_AT:
                    unit_max(c, SCORES_AT[s])
                if s in VALUES_AT:
                    unit_gate(c, VALUES_AT[s])

            def chunk(c, last):
                for i in range(NW):
                    name = TILES[i] if i < NT else None
                    attention(c, step_of(i, 0))
                    if name == "p1":
                        pooled_diff(c, 0)
                    if name in ("q0", "q1"):
                        split_w(c, i + 2)
                    if 1 <= i < NT:
                        evacuate(c, i)
                    if name and name[0] == "p":
                        mix_p_gate(c, int(name[1]))
                    if i == NT + 3:
                        first_half_sums(c, last)
                    elif name not in ("q0", "q1"):
                        for w in splits_behind(i, last):
                            split_w(c, w, last)
                    if i == 1:
                        evacuate(c, 0)
                    if name in POOLED_AT:
                        pooled_diff(c, POOLED_AT[name])
                    attention(c, step_of(i, 1))
                    if i == 3:
                        split_values(c)
                nc.vector.memset(prev_mask[:, :], 0.0).then_inc(mask_reset, 1)
                dve.wait_ge(window_step, c * NWIN + NWIN)
                nc.vector.memset(corr[:, :, :], 1.0).then_inc(corr_reset, 1)
                if last:
                    for tt in range(BLOCKS):
                        residual(c, 1, tt)
                        statistics(c, 1, tt)
                        norm_scalars(c, tt)
                        if tt < BLOCKS - 1:
                            centre(c, tt)
                    halves = [slice(h * CH, (h + 1) * CH) for h in range(2)]
                    for cols in halves:
                        centre(c, tt, cols)
                    dve.wait_ge(rstd_ready, c * BLOCKS + tt + 1)
                    for h, cols in enumerate(halves):
                        dve.wait_ge(centred, c * BLOCKS + tt + h + 1)
                        stt(out=resid[:, tt, cols], in0=resid[:, tt, cols], scalar=rstd[:, tt:tt + 1],
                            in1=ln_b_sb[:, cols], op0=ALU.mult, op1=ALU.add).then_inc(ln_done[tt], 1)
                    return
                for tt in range(BLOCKS):
                    residual(c, 1, tt)
                    statistics(c, 1, tt)
                    if tt:
                        norm_scalars(c, tt - 1)
                split_w(c, NW + 1)
                norm_scalars(c, BLOCKS - 1)
                for tt in range(BLOCKS):
                    centre(c, tt)
                    if tt == 0:
                        split_w(c, NW + 2)

            with dve.Fori(0, CHUNKS - 1) as c:
                chunk(c, False)
            chunk(CHUNKS - 1, True)

        @block.gpsimd
        def _(pool):
            tt_ = nc.gpsimd.tensor_tensor

            nc.gpsimd.memset(k_hi2[:, :, :].bitcast(F32), 0.0).then_inc(keys_cleared, 1)
            nc.gpsimd.memset(k_lo2[:, :, :].bitcast(F32), 0.0)
            nc.gpsimd.memset(v2[:, :, :, :].bitcast(F32), 0.0)
            nc.gpsimd.memset(u_ext[:, :, CH:CH + HALO], 0.0)
            nc.gpsimd.memset(minus_half[:, :], -0.5).then_inc(cleared, 1)
            pool.wait_ge(cleared, 1)

            pool.wait_ge(tables_loaded, TABLES * 16)

            def window_sums(c, g):
                n = POOL_ORDER.index(g)
                pool.wait_ge(hi_ready, c * NT + TILES.index(f"u{g}") + 1)
                if n:
                    pool.wait_ge(pooled_ready, c * GROUPS + n)
                steps = WINDOW_STEPS[g]
                src, lo = u_ext[:, g, :], 0
                for k in range(steps):
                    d = 1 << k
                    lo += d
                    start = HALO if k == steps - 1 else lo
                    dst = win[(steps + 1 + (steps - 1 - k)) % 2]
                    if k:
                        pool.wait_ge(window_step, c * NWIN + window_count(g, k))
                    tt_(out=dst[:, start:], in0=src[:, start:], in1=src[:, start - d:HALO + CH - d],
                        op=ALU.add).then_inc(window_step, 1)
                    src = dst
                pool.wait_ge(window_step, c * NWIN + window_count(g, steps))
                pool.wait_ge(corr_reset, c + 1)
                tt_(out=src[:, HALO:2 * HALO], in0=src[:, HALO:2 * HALO], in1=corr[:, g, :],
                    op=ALU.mult).then_inc(window_step, 1)

            def pooled_part(c, g):
                n = POOL_ORDER.index(g)
                pool.wait_ge(pooled_high, c * GROUPS + n + 1)
                tt_(out=pooled_lo[:, :], in0=pooled[:, :], in1=pooled_hi[:, :].bitcast(F32),
                    op=ALU.subtract).then_inc(pooled_split, 1)

            def mix_p_part(c, g):
                n = POOL_ORDER.index(g)
                pool.wait_ge(mix_p_high, c * GROUPS + n + 1)
                tt_(out=mix_lo[:, g, :], in0=mix_p[:, :], in1=mix_hi[:, g, :].bitcast(F32),
                    op=ALU.subtract).then_inc(mix_p_split, 1)

            def split_x(c, k):
                pool.wait_ge(x_high, c * KT + k + 1)
                tt_(out=x_lo[:, k, :], in0=x_stage[:, k % NX, :], in1=x_hi[:, k, :].bitcast(F32),
                    op=ALU.subtract).then_inc(x_split, 1)

            def deviation(c, tt):
                pool.wait_ge(var_ready, c * BLOCKS + tt + 1)
                tt_(out=rstd[:, tt:tt + 1], in0=var_eps[:, tt:tt + 1], in1=minus_half[:, 0:1],
                    op=ALU.pow).then_inc(rstd_ready, 1)

            def offset(c, tt):
                if tt == 0:
                    pool.wait_ge(ln_loaded, 2 * 16)
                pool.wait_ge(scaled, c * BLOCKS + tt + 1)
                tt_(out=resid[:, tt, :], in0=resid[:, tt, :], in1=ln_b_sb[:, :], op=ALU.add).then_inc(ln_done[tt], 1)

            def unit_band(c, n):
                if n:
                    pool.wait_ge(av_ready, c * NU + n)
                pool.wait_ge(t_high, c * (NU + 1) + n + 2)
                shape = [P, 2, GQ, P]
                mask = masks[:, :, :].unsqueeze(2).broadcast_to(shape)
                tt_(out=band_hi[:, :, :, :], in0=pt_hi[:, :, :].bitcast(F32).unsqueeze(1).broadcast_to(shape),
                    in1=mask, op=ALU.mult).then_inc(band_hi_ready, 1)
                pool.wait_ge(t_low, c * (NU + 1) + n + 2)
                tt_(out=band_lo[:, :, :, :], in0=pt_lo[:, :, :].bitcast(F32).unsqueeze(1).broadcast_to(shape),
                    in1=mask, op=ALU.mult).then_inc(band_lo_ready, 1)

            def unit_mix(c, n):
                b, g = UNITS[n]
                at = (slice(None), slice(4 + 2 * g, 6 + 2 * g), slice(b * P, (b + 1) * P))
                pool.wait_ge(mix_a_high, c * NU + n + 1)
                tt_(out=mix_lo[at], in0=mix_a[:, :, :], in1=mix_hi[at].bitcast(F32),
                    op=ALU.subtract).then_inc(mix_a_split, 1)

            def attention(c, s):
                if s is None:
                    return
                if s in TRANSPOSE_AT:
                    unit_band(c, TRANSPOSE_AT[s])
                if s in MIX_AT:
                    unit_mix(c, MIX_AT[s])

            def chunk(c, last):
                for i in range(NW):
                    name = TILES[i] if i < NT else None
                    attention(c, step_of(i, 0))
                    if name == "p1":
                        pooled_part(c, 0)
                    if name == "p0":
                        mix_p_part(c, 0)
                    attention(c, step_of(i, 1))
                    if name in POOLED_AT:
                        pooled_part(c, POOLED_AT[name])
                    if name in ("p3", "p2", "p1"):
                        mix_p_part(c, int(name[1]))
                    if name and name[0] == "u":
                        window_sums(c, int(name[1]))
                    if not last and i >= NT:
                        split_x(c + 1, i - NT)
                for tt in range(BLOCKS):
                    deviation(c, tt)
                    if last and tt < BLOCKS - 1:
                        offset(c, tt)
                if not last:
                    for tt in range(BLOCKS):
                        offset(c, tt)

            with pool.Fori(0, CHUNKS - 1) as c:
                chunk(c, False)
            chunk(CHUNKS - 1, True)


def shape_constants():
    import numpy as np

    m = np.arange(BIAS_ROW)
    dist = 2 * P - 1 - m
    valid = (dist >= 0) & (dist < P)
    exact = BUCKETS // 2
    far = np.log(np.maximum(dist, 1).astype(np.float32) / exact) / np.log(P / exact) * (BUCKETS - exact)
    bucket = np.where(dist < exact, dist, np.minimum(exact + far.astype(np.int32), BUCKETS - 1))
    onehot = np.zeros((BUCKETS + 1, BIAS_ROW), np.float32)
    onehot[bucket[valid], m[valid]] = 1.0
    onehot[BUCKETS, ~valid] = NEG_INF
    key, query = np.arange(P)[:, None], np.arange(P)[None, :]
    masks = np.stack([key > query, key <= query], 1).astype(np.float32)
    windows = 2.0 ** np.arange(1, GROUPS + 1)[:, None]
    counts = np.minimum(np.arange(HALO)[None, :] + 1, windows)
    first = np.broadcast_to((windows / counts).astype(np.float32), (P, GROUPS, HALO))
    return onehot, np.eye(P, dtype=np.float32), masks, np.ascontiguousarray(first)


def kernel(x, ln_g, ln_b, w_in, pool_w, pool_scale, sinks, w_out, rel_bias):
    import numpy as np
    import concourse.bacc as bacc
    from concourse.bass_utils import run_bass_kernel_spmd

    x, w_in, w_out = np.asarray(x)[0], np.asarray(w_in)[0], np.asarray(w_out)[0]
    order = {"u": 0, "p": 4, "q": 8, "k": 12, "v": 13, "a": 14}
    tiles = w_in.reshape(KT, P, -1, P).transpose(2, 1, 0, 3)
    tiles = [tiles[order[t[0]] + int(t[1:] or 0)].reshape(P, D) for t in TILES]
    slots = w_out.reshape(KT // 2, 2, P, 2, CH).transpose(3, 0, 2, 1, 4)
    slots = [slots[n, kp].reshape(P, D) for n, kp in SLOTS]
    onehot, identity, masks, first = shape_constants()
    arrays = {
        "x_t": x.reshape(CHUNKS, CH, KT, P).transpose(0, 3, 2, 1),
        "x_rows": x.reshape(CHUNKS, BLOCKS, P, D),
        "weights": np.stack(tiles + slots),
        "pool_w": np.asarray(pool_w)[0].transpose(1, 0, 2),
        "pool_scale": np.asarray(pool_scale)[0].reshape(GROUPS, P).T,
        "sinks": np.broadcast_to(np.asarray(sinks)[0], (P, HEADS)),
        "rel_bias": np.asarray(rel_bias),
        "ln_g": np.broadcast_to(np.asarray(ln_g)[0], (P, D)),
        "ln_b": np.broadcast_to(np.asarray(ln_b)[0], (P, D)),
        "buckets": onehot,
        "identity": identity,
        "band_masks": masks,
        "first_counts": first,
    }
    arrays = {n: np.ascontiguousarray(a) for n, a in arrays.items()}
    nc = bacc.Bacc("TRN2", target_bir_lowering=False, num_devices=1, dynamic_dma_scratch_size=1024)
    args = [nc.dram_tensor(n, a.shape, F32, kind="ExternalInput").ap() for n, a in arrays.items()]
    args.append(nc.dram_tensor("scratch", (HEADS * P * BIAS_ROW,), F32, kind="Internal").ap())
    args.append(nc.dram_tensor("out", (CHUNKS, BLOCKS, P, D), F32, kind="ExternalOutput").ap())
    hybrid_layer(nc, *args)
    r = run_bass_kernel_spmd(nc, [arrays], core_ids=[0])
    return r.results[0]["out"].reshape(1, SEQ, D)
```
